# Optimizing a Trainium2 kernel written in Bass

```python
import math
import jax, jax.numpy as jnp
from jax import lax
import numpy as np

D_MODEL = 1024
BATCH = 1
SEQ = 1024
DEPTH = 2

N_MIXERS = 2
HEAD_DIM = 64
ROPE_THETA = 500000.0
ROT_DIM = HEAD_DIM // 4

DIL_GROUPS = ((128, 1), (512, 4), (2048, 16))
DIL_HEADS = 4
N_DIL_HEADS = len(DIL_GROUPS) * DIL_HEADS
DIL_WIDTH = N_DIL_HEADS * HEAD_DIM
WIN_BLOCK = 64

MEM_LEN = 256
MEM_HEADS = 4
MEM_WIDTH = MEM_HEADS * HEAD_DIM

MLA_HEADS = 8
MLA_NOPE = 64
MLA_ROPE = 32
MLA_V = 64
Q_LORA = 256
KV_LORA = 128
MLA_Q_BLOCK = 128

N_GROUPS = 4
EXPERTS_PER_GROUP = 8
N_EXPERTS = N_GROUPS * EXPERTS_PER_GROUP
TOP_K = 2
D_EXPERT = 512
MOE_BLOCK = 128

LN_EPS = 1e-5
RMS_EPS = 1e-6
NEG_INF = -1e30
ALPHA = (2 * DEPTH) ** 0.25
BETA = (8 * DEPTH) ** -0.25
N_A_LAYERS = (DEPTH + 1) // 2
N_B_LAYERS = DEPTH // 2

A_IN_WIDTH = 3 * DIL_WIDTH + MEM_WIDTH
B_IN_WIDTH = Q_LORA + KV_LORA + MLA_ROPE + MEM_WIDTH
A_OUT_IN = DIL_HEADS * HEAD_DIM + MEM_WIDTH
B_OUT_IN = MLA_HEADS * MLA_V + MEM_WIDTH

kernel_name = "hybrid_dilated_mla_hmoe_encoder"

def layer_norm(x, g, b):
    xf = x.astype(jnp.float32)
    mu = xf.mean(-1, keepdims=True)
    var = jnp.square(xf - mu).mean(-1, keepdims=True)
    return ((xf - mu) * lax.rsqrt(var + LN_EPS) * g + b).astype(x.dtype)

def rms_norm(x, g):
    xf = x.astype(jnp.float32)
    return (xf * lax.rsqrt(jnp.square(xf).mean(-1, keepdims=True) + RMS_EPS) * g).astype(x.dtype)

def rope_tables(seq, dim):
    inv = ROPE_THETA ** (-jnp.arange(0, dim, 2, dtype=jnp.float32) / dim)
    ang = jnp.arange(seq, dtype=jnp.float32)[:, None] * inv[None, :]
    return jnp.cos(ang), jnp.sin(ang)

def apply_rope(t, cos, sin):
    half = t.shape[-1] // 2
    tf = t.astype(jnp.float32)
    t1, t2 = tf[..., :half], tf[..., half:]
    c, s = cos[None, :, None, :], sin[None, :, None, :]
    return jnp.concatenate([t1 * c - t2 * s, t2 * c + t1 * s], -1).astype(t.dtype)

def partial_rope(t, cos, sin):
    return jnp.concatenate([apply_rope(t[..., :ROT_DIM], cos, sin), t[..., ROT_DIM:]], -1)

def banded_attention(q, k, v, radius):
    n, L, h, dh = q.shape
    blk = WIN_BLOCK
    nb = -(-L // blk)
    Lp = nb * blk
    qb = jnp.pad(q, ((0, 0), (0, Lp - L), (0, 0), (0, 0))).reshape(n, nb, blk, h, dh)
    kv_pad = ((0, 0), (blk, Lp - L + blk), (0, 0), (0, 0))
    kp = jnp.pad(k, kv_pad).reshape(n, nb + 2, blk, h, dh)
    vp = jnp.pad(v, kv_pad).reshape(n, nb + 2, blk, h, dh)
    kw = jnp.concatenate([kp[:, :-2], kp[:, 1:-1], kp[:, 2:]], axis=2)
    vw = jnp.concatenate([vp[:, :-2], vp[:, 1:-1], vp[:, 2:]], axis=2)
    qpos = jnp.arange(nb)[:, None] * blk + jnp.arange(blk)[None, :]
    kpos = jnp.arange(nb)[:, None] * blk - blk + jnp.arange(3 * blk)[None, :]
    mask = ((jnp.abs(qpos[:, :, None] - kpos[:, None, :]) <= radius)
            & (kpos[:, None, :] >= 0) & (kpos[:, None, :] < L))
    s = jnp.einsum('nbqhd,nbkhd->nbhqk', qb, kw, preferred_element_type=jnp.float32) * (dh ** -0.5)
    s = jnp.where(mask[None, :, None], s, NEG_INF)
    lse = jax.nn.logsumexp(s, axis=-1)
    p = jnp.exp(s - lse[..., None])
    o = jnp.einsum('nbhqk,nbkhd->nbqhd', p.astype(v.dtype), vw)
    o = o.reshape(n, Lp, h, dh)[:, :L]
    lse = lse.transpose(0, 1, 3, 2).reshape(n, Lp, h)[:, :L]
    return o, lse

def dilated_mixer(q, k, v):
    B, S = q.shape[0], q.shape[1]
    outs, lses = [], []
    for g, (window, dil) in enumerate(DIL_GROUPS):
        sl = slice(g * DIL_HEADS, (g + 1) * DIL_HEADS)
        T = S // dil
        radius = window // (2 * dil)

        def to_sub(t):
            return t[:, :, sl].reshape(B, T, dil, DIL_HEADS, HEAD_DIM).transpose(0, 2, 1, 3, 4).reshape(B * dil, T, DIL_HEADS, HEAD_DIM)

        o, lse = banded_attention(to_sub(q), to_sub(k), to_sub(v), radius)
        outs.append(o.reshape(B, dil, T, DIL_HEADS, HEAD_DIM).transpose(0, 2, 1, 3, 4).reshape(B, S, DIL_HEADS, HEAD_DIM))
        lses.append(lse.reshape(B, dil, T, DIL_HEADS).transpose(0, 2, 1, 3).reshape(B, S, DIL_HEADS))
    w = jax.nn.softmax(jnp.stack(lses), axis=0)
    return jnp.einsum('gbsh,gbshd->bshd', w.astype(q.dtype), jnp.stack(outs))

def mla_mixer(c_q, c_kv, k_rope, q_norm_g, w_qb, kv_norm_g, w_kvb, cos, sin):
    B, S = c_q.shape[0], c_q.shape[1]
    q = (rms_norm(c_q, q_norm_g) @ w_qb).reshape(B, S, MLA_HEADS, MLA_NOPE + MLA_ROPE)
    q_nope = q[..., :MLA_NOPE]
    q_pe = apply_rope(q[..., MLA_NOPE:], cos, sin)
    kv = (rms_norm(c_kv, kv_norm_g) @ w_kvb).reshape(B, S, MLA_HEADS, MLA_NOPE + MLA_V)
    k_nope, v = kv[..., :MLA_NOPE], kv[..., MLA_NOPE:]
    k_pe = apply_rope(k_rope[:, :, None, :], cos, sin)[:, :, 0]
    scale = (MLA_NOPE + MLA_ROPE) ** -0.5
    nq = S // MLA_Q_BLOCK
    qn_b = q_nope.reshape(B, nq, MLA_Q_BLOCK, MLA_HEADS, MLA_NOPE).transpose(1, 0, 2, 3, 4)
    qp_b = q_pe.reshape(B, nq, MLA_Q_BLOCK, MLA_HEADS, MLA_ROPE).transpose(1, 0, 2, 3, 4)

    def one_block(args):
        qn, qp = args
        s = (jnp.einsum('bqhd,bkhd->bhqk', qn, k_nope, preferred_element_type=jnp.float32)
             + jnp.einsum('bqhr,bkr->bhqk', qp, k_pe, preferred_element_type=jnp.float32)) * scale
        p = jax.nn.softmax(s, axis=-1)
        return jnp.einsum('bhqk,bkhd->bqhd', p.astype(v.dtype), v)

    o = lax.map(one_block, (qn_b, qp_b))
    return o.transpose(1, 0, 2, 3, 4).reshape(B, S, MLA_HEADS, MLA_V)

def memory_attention(q, mem, w_kv):
    B, M = mem.shape[0], mem.shape[1]
    kv = (mem @ w_kv).reshape(B, M, 2, MEM_HEADS, HEAD_DIM)
    k, v = kv[:, :, 0], kv[:, :, 1]
    s = jnp.einsum('bshd,bmhd->bhsm', q, k, preferred_element_type=jnp.float32) * (HEAD_DIM ** -0.5)
    p = jax.nn.softmax(s, axis=-1)
    return jnp.einsum('bhsm,bmhd->bshd', p.astype(v.dtype), v)

def hierarchical_moe(x, w_grp, b_grp, w_exp_router, b_exp, w_gate, w_up, w_down):
    B, S, D = x.shape
    xt = x.reshape(-1, D)
    n = xt.shape[0]
    grp_logits = (xt @ w_grp).astype(jnp.float32) + b_grp
    g_idx = jnp.argmax(grp_logits, axis=-1)
    g_gate = jnp.take_along_axis(jax.nn.softmax(grp_logits, axis=-1), g_idx[:, None], axis=-1)
    exp_logits = ((xt @ w_exp_router).astype(jnp.float32) + b_exp).reshape(n, N_GROUPS, EXPERTS_PER_GROUP)
    in_grp = jnp.take_along_axis(exp_logits, g_idx[:, None, None], axis=1)[:, 0]
    top_v, top_i = lax.top_k(in_grp, TOP_K)
    gates = jax.nn.softmax(top_v, axis=-1) * g_gate
    eid = (g_idx[:, None] * EXPERTS_PER_GROUP + top_i).reshape(-1).astype(jnp.int32)
    a = n * TOP_K
    tok = jnp.arange(a, dtype=jnp.int32) // TOP_K
    gw = gates.reshape(-1)
    order = jnp.argsort(eid)
    eid_s, tok_s, gw_s = eid[order], tok[order], gw[order]
    counts = jnp.zeros((N_EXPERTS,), jnp.int32).at[eid].add(1)
    starts = jnp.cumsum(counts) - counts
    padded = (counts + MOE_BLOCK - 1) // MOE_BLOCK * MOE_BLOCK
    pends = jnp.cumsum(padded)
    pstarts = pends - padded
    dest = pstarts[eid_s] + (jnp.arange(a, dtype=jnp.int32) - starts[eid_s])
    n_slots = (-(-a // MOE_BLOCK) + N_EXPERTS) * MOE_BLOCK
    n_blocks = n_slots // MOE_BLOCK
    slot_tok = jnp.zeros((n_slots,), jnp.int32).at[dest].set(tok_s)
    slot_w = jnp.zeros((n_slots,), jnp.float32).at[dest].set(gw_s)
    blk_expert = jnp.minimum(jnp.searchsorted(pends, jnp.arange(n_blocks, dtype=jnp.int32) * MOE_BLOCK, side='right'), N_EXPERTS - 1)
    xs = xt[slot_tok].reshape(n_blocks, MOE_BLOCK, D)

    def expert_block(args):
        xb, e = args
        h = jax.nn.silu(xb @ w_gate[e]) * (xb @ w_up[e])
        return h @ w_down[e]

    ys = lax.map(expert_block, (xs, blk_expert)).reshape(n_slots, D)
    out = jax.ops.segment_sum(ys * slot_w[:, None].astype(ys.dtype), slot_tok, num_segments=n)
    return out.reshape(B, S, D)

def setup_inputs(seed: int = 0) -> dict:
    key = jax.random.key(seed)
    ks = iter(jax.random.split(key, 32))

    def nrm(shape, scale):
        return jax.random.normal(next(ks), shape, jnp.float32) * scale

    D = D_MODEL
    return {
        "x": nrm((BATCH, SEQ, D), 1.0),
        "mem": nrm((BATCH, MEM_LEN, D), 1.0),
        "a_w_in": nrm((N_A_LAYERS, D, A_IN_WIDTH), D ** -0.5),
        "a_w_out": nrm((N_A_LAYERS, A_OUT_IN, D), A_OUT_IN ** -0.5 * BETA),
        "b_w_in": nrm((N_B_LAYERS, D, B_IN_WIDTH), D ** -0.5),
        "b_q_norm": 1.0 + nrm((N_B_LAYERS, Q_LORA), 0.02),
        "b_w_qb": nrm((N_B_LAYERS, Q_LORA, MLA_HEADS * (MLA_NOPE + MLA_ROPE)), Q_LORA ** -0.5),
        "b_kv_norm": 1.0 + nrm((N_B_LAYERS, KV_LORA), 0.02),
        "b_w_kvb": nrm((N_B_LAYERS, KV_LORA, MLA_HEADS * (MLA_NOPE + MLA_V)), KV_LORA ** -0.5),
        "b_w_out": nrm((N_B_LAYERS, B_OUT_IN, D), B_OUT_IN ** -0.5 * BETA),
        "mem_w_kv": nrm((DEPTH, D, 2 * MEM_WIDTH), D ** -0.5),
        "ln_mix_g": 1.0 + nrm((DEPTH, D), 0.02),
        "ln_mix_b": nrm((DEPTH, D), 0.02),
        "ln_ffn_g": 1.0 + nrm((DEPTH, D), 0.02),
        "ln_ffn_b": nrm((DEPTH, D), 0.02),
        "router_w_grp": nrm((DEPTH, D, N_GROUPS), D ** -0.5),
        "router_b_grp": nrm((DEPTH, N_GROUPS), 0.01),
        "router_w_exp": nrm((DEPTH, D, N_EXPERTS), D ** -0.5),
        "router_b_exp": nrm((DEPTH, N_EXPERTS), 0.01),
        "exp_w_gate": nrm((DEPTH, N_EXPERTS, D, D_EXPERT), D ** -0.5),
        "exp_w_up": nrm((DEPTH, N_EXPERTS, D, D_EXPERT), D ** -0.5),
        "exp_w_down": nrm((DEPTH, N_EXPERTS, D_EXPERT, D), D_EXPERT ** -0.5 * BETA),
    }

def reference(x, mem, a_w_in, a_w_out, b_w_in, b_q_norm, b_w_qb, b_kv_norm, b_w_kvb, b_w_out,
              mem_w_kv, ln_mix_g, ln_mix_b, ln_ffn_g, ln_ffn_b, router_w_grp, router_b_grp,
              router_w_exp, router_b_exp, exp_w_gate, exp_w_up, exp_w_down):
    B, S, _ = x.shape
    cos_a, sin_a = rope_tables(S, ROT_DIM)
    cos_b, sin_b = rope_tables(S, MLA_ROPE)
    for i in range(DEPTH):
        j = i // N_MIXERS
        if i % N_MIXERS == 0:
            proj = x @ a_w_in[j]
            q, k, v, qm = jnp.split(proj, [DIL_WIDTH, 2 * DIL_WIDTH, 3 * DIL_WIDTH], axis=-1)
            q = partial_rope(q.reshape(B, S, N_DIL_HEADS, HEAD_DIM), cos_a, sin_a)
            k = partial_rope(k.reshape(B, S, N_DIL_HEADS, HEAD_DIM), cos_a, sin_a)
            v = v.reshape(B, S, N_DIL_HEADS, HEAD_DIM)
            mix = dilated_mixer(q, k, v).reshape(B, S, DIL_HEADS * HEAD_DIM)
            w_out = a_w_out[j]
        else:
            proj = x @ b_w_in[j]
            c_q, c_kv, k_rope, qm = jnp.split(proj, [Q_LORA, Q_LORA + KV_LORA, Q_LORA + KV_LORA + MLA_ROPE], axis=-1)
            mix = mla_mixer(c_q, c_kv, k_rope, b_q_norm[j], b_w_qb[j], b_kv_norm[j], b_w_kvb[j],
                            cos_b, sin_b).reshape(B, S, MLA_HEADS * MLA_V)
            w_out = b_w_out[j]
        mo = memory_attention(qm.reshape(B, S, MEM_HEADS, HEAD_DIM), mem, mem_w_kv[i]).reshape(B, S, MEM_WIDTH)
        y = jnp.concatenate([mix, mo], axis=-1) @ w_out
        x = layer_norm(ALPHA * x + y, ln_mix_g[i], ln_mix_b[i])
        f = hierarchical_moe(x, router_w_grp[i], router_b_grp[i], router_w_exp[i], router_b_exp[i],
                             exp_w_gate[i], exp_w_up[i], exp_w_down[i])
        x = layer_norm(ALPHA * x + f, ln_ffn_g[i], ln_ffn_b[i])
    return x


_drawn_inputs = setup_inputs


def setup_inputs(seed=0):
    import zlib

    import numpy as np

    out = dict(_drawn_inputs(seed))
    spreads = {}
    factors = {'b_q_norm': 8.0, 'b_kv_norm': 8.0, 'router_b_grp': 7.754, 'router_b_exp': 7.27}
    for name, (base, spread) in spreads.items():
        noise = np.random.default_rng([zlib.crc32(name.encode()), seed]).standard_normal(out[name].shape)
        drawn = base * np.exp(spread * noise) if base else spread * noise
        out[name] = __import__('jax').numpy.asarray(drawn.astype(out[name].dtype))
    for name, factor in factors.items():
        out[name] = (out[name] * factor).astype(out[name].dtype)
    return out
```

```python
import numpy as np
from contextlib import ExitStack

import concourse.bass as bass
from concourse import mybir

F32 = mybir.dt.float32
I32 = mybir.dt.int32
ALU = mybir.AluOpType
ACT = mybir.ActivationFunctionType
AX = mybir.AxisListType

P = 128
D = 1024
S = 1024
DEPTH = 2
KT = D // P
TT = S // P
HALF = 512
DH = 64
DIL_GROUPS = ((128, 1), (512, 4), (2048, 16))
NG = len(DIL_GROUPS)
GH = 4
GW = GH * DH
PADW = S + 2 * DH
MEM = 256
MLA_H = 8
QL, KVL, ROPE_B = 256, 128, 32
LAT = QL + KVL + ROPE_B
QKB = DH + ROPE_B
N_GRP, EPG = 4, 8
NE = N_GRP * EPG
NR = N_GRP + NE
DE = 512
ALPHA = (2 * DEPTH) ** 0.25
LN_EPS, RMS_EPS = 1e-5, 1e-6
SCALE_A = DH ** -0.5
SCALE_B = QKB ** -0.5
ROPE_THETA = 500000.0
BIG = 1e30
LOWEST = -3e38

CAP = 104
NOVER = (2 * S) // (CAP + 1)
NCHUNK = S // CAP
SLOTS = (NE + NOVER) * CAP
NOWHERE = 1 << 20
OSTR = GW + 2 * GH
PART = 4096


def build(nc, io):
    with ExitStack() as ctx:
        def sb(name, shape, dt=F32):
            return ctx.enter_context(nc.sbuf_tensor(name, shape, dt))

        def sem(name):
            return ctx.enter_context(nc.semaphore(name))

        ring = sb("ring", [P, 6 * PART])
        arena = sb("arena", [P, 88 * 256])
        o_stage = sb("o_stage", [P, 2, OSTR])
        km_t = sb("mem_keys_t", [P, 2, MEM])
        v_mem = sb("mem_values", [P, 2, GW])
        q_stage = sb("q_stage", [P, 2, GH, P])
        ln_gb = sb("ln_gb", [P, 2, D])
        ident = sb("ident", [P, P])
        tri = sb("tri", [P, P])
        ones = sb("ones", [P, P])
        w_router = sb("w_router", [P, KT, NR])
        b_router = sb("b_router", [P, NR])
        stat = sb("max_and_sum", [P, 2, 2, GH])
        neg_max = sb("neg_max", [P, 2, GH])
        recip_den = sb("recip_den", [P, 2, GH])
        stats = sb("ln_stats", [P, 2, 2, 6])
        mean_var = sb("ln_mean_var", [P, TT, 2])
        std = sb("ln_std", [P, TT])
        rstd = sb("ln_rstd", [P, TT, 2])
        eps = sb("eps", [P, 2])
        gates = sb("gates", [P, TT, 2])
        slots_i = sb("slots_i", [P, TT, 2], I32)
        infos = sb("infos", [P, TT, 2, 2], I32)
        g_idx = sb("gather_idx", [P, 2, 2], I32)
        s_idx = sb("scatter_idx", [P, 2, 2], I32)
        over_i = sb("over_table", [P, NOVER + 1], I32)
        rms_ss = sb("rms_ss", [P, TT, 2])
        rms_g = sb("rms_g", [P, 3])
        merge_e = sb("merge_e", [P, TT, NG, GH])
        merge_m = sb("merge_m", [P, TT, GH])
        logits = sb("logits", [P, TT, NR])

        ps = ctx.enter_context(nc.psum_tensor("banks", [P, 8, HALF], F32))

        def at(kb, *shape, rows=P, base=arena):
            n = int(np.prod(shape))
            off = int(kb * 256)
            v = base[0:rows, off:off + n]
            if len(shape) == 1:
                return v
            names = "abcd"[:len(shape)]
            return v.rearrange(f"p ({' '.join(names)}) -> p {' '.join(names)}",
                               **{c: s for c, s in zip(names, shape)})

        def ring_at(kb, *shape):
            return at(kb, *shape, base=ring)

        X = at(0, TT, D)
        XT = at(32, KT, S)
        q_t = at(32, 2, S)
        k_t = at(40, 2, PADW)
        v_a = at(49, 9, GW)
        merged = at(32, TT, NG, OSTR)
        qm_t = at(64, 2, S)
        masked_by = at(60, 2, 256)
        prob = at(72, 2, S)
        prob_t = at(80, 2, S)
        rope_a = at(72, 2, S)
        rope_tmp = at(80, 4, HALF)
        x_t = [ring_at(0, KT, PADW), ring_at(36, KT, PADW)]
        w_a = [ring_at(72, 3, KT, GW), at(0, 3, KT, GW)]
        w_qm_a = at(24, KT, GW)
        mem_w = [at(0, KT, 2 * GW), ring_at(32, KT, 2 * GW)]
        mem_t = [at(16, KT, MEM), ring_at(88, KT, MEM)]
        w_out = [ring_at(80, 4, D), ring_at(64, 6, D)]
        mix = [ring_at(0, TT, 512), ring_at(0, TT, 768)]
        w_in_b = ring_at(0, KT, LAT + GW)
        rope_b = ring_at(24, 2, S)
        q_head = ring_at(32, 2, S)
        k_head = ring_at(40, 2, S)
        w_q_head = ring_at(48, 2, 2, QKB)
        w_k_head = ring_at(49.5, 2, DH)
        w_v = ring_at(50, MLA_H, DH)
        rope_tmp_b = ring_at(52, 2, HALF)
        latent = at(72, TT, LAT)
        v_b = at(32, TT, MLA_H * DH)
        cq_t = at(48, 2, S)
        ckv_t = at(56, S)
        k_rot = at(60, S)
        square = at(85, 2, QL + KVL)
        mix_t = at(72, 2, 6, P)
        xs = at(32, 2, D)
        xs_t = [at(40, KT, CAP), at(44, KT, CAP)]
        h_t = [at(48, 4, CAP), at(50, 4, CAP)]
        sil = [at(52, 4, CAP), at(54, 4, CAP)]
        ys = at(56, 2, D)
        y_in = at(64, 2, 2, D)

        og = nc.dram_tensor("group_results", [NG, S, OSTR], F32).ap()
        x1_d = [nc.dram_tensor(f"moe_in_{l}", [S, D], F32).ap() for l in range(DEPTH)]
        slot_d = [nc.dram_tensor(f"slot_info_{l}", [SLOTS, 2], I32).ap() for l in range(DEPTH)]
        y_d = [nc.dram_tensor(f"expert_out_{l}", [2 * S, D], F32).ap() for l in range(DEPTH)]

        consts_in = sem("consts_in")
        infos_in = sem("infos_in")
        zeroed = sem("zeroed")
        fenced = {e: sem(f"fenced_{n}") for e, n in ((nc.sync.engine, "sp"), (nc.gpsimd.engine, "pool"), (nc.vector.engine, "dve"))}
        slots_cleared = sem("slots_cleared")
        mem_in = sem("mem_in")
        mem_proj = sem("mem_proj")
        mem_kv_act = sem("mem_kv_act")
        mem_kv_dve = sem("mem_kv_dve")
        x_in = [sem("x_in0"), sem("x_in1")]
        w_in = [sem("w_in0"), sem("w_in1")]
        rope_in = sem("rope_in")
        wqm_in = sem("wqm_in")
        act_full = sem("proj_for_act")
        act_free = sem("proj_freed_by_act")
        dve_full = sem("proj_for_dve")
        dve_free = sem("proj_freed_by_dve")
        rope_a_s = sem("rope_shuffled")
        rope_b_s = sem("rope_cos")
        rope_c_s = sem("rope_sin")
        q_staged = sem("q_staged")
        mask_in = [sem("mask_in0"), sem("mask_in1")]
        scores = sem("scores")
        masked = sem("masked")
        max_ready = sem("max_ready")
        stat_kept = sem("stat_kept")
        probs = sem("probs")
        probs_t = sem("probs_transposed")
        pt_act = sem("pt_copied_act")
        pt_dve = sem("pt_copied_dve")
        pv = sem("pv")
        o_out = sem("o_out")
        o_stored = [sem("o_stored0"), sem("o_stored1")]
        mask_zero = sem("mask_zero")
        den_ready = sem("den_ready")
        merge_in = sem("merge_in")
        mstep = sem("merge_step")
        merge_diff = sem("merge_diff")
        merge_exp = sem("merge_exp")
        mix_done = sem("mix_done")
        x_res_in = sem("x_res_in")
        wout_in = sem("wout_in")
        gb_in = sem("gb_in")
        router_in = sem("router_in")
        mixt_ps = sem("mixt_ps")
        mixt_act = sem("mixt_act")
        y_ps = sem("y_ps")
        z_done = sem("z_done")
        st_done = sem("stats_done")
        mv_done = sem("mean_var_done")
        sd_done = sem("std_done")
        rs_step = sem("rstd_step")
        rs_done = sem("rstd_done")
        norm_done = sem("norm_done")
        gmul_done = sem("gmul_done")
        x_ready = sem("x_ready")
        xt_ps = sem("xt_ps")
        xt_act = sem("xt_act")
        xt_dve = sem("xt_dve")
        r_ps = sem("router_ps")
        r_out = sem("router_out")
        x1_stored = sem("x1_stored")
        rstep = sem("routing_step")
        route_exp_in = sem("route_exp_in")
        route_exp = sem("route_exp")
        route_hot = sem("route_hot")
        rank_ps = sem("rank_ps")
        route_done = sem("route_done")
        table_in = sem("table_in")
        slots_sent = sem("slots_sent")
        ring_in = [sem(f"ring_in{i}") for i in range(6)]
        gi_in = [sem("gather_idx_in0"), sem("gather_idx_in1")]
        si_in = [sem("scatter_idx_in0"), sem("scatter_idx_in1")]
        xs_in = [sem("xs_in0"), sem("xs_in1")]
        xst_ps = sem("xst_ps")
        xst_out = sem("xst_out")
        gate_ps = sem("gate_ps")
        up_ps = sem("up_ps")
        silu_done = sem("silu_done")
        h_done = sem("h_done")
        down_ps = sem("down_ps")
        y_act = sem("y_act")
        y_dve = sem("y_dve")
        ys_out = [sem("ys_out0"), sem("ys_out1")]
        yin = [sem("y_in0"), sem("y_in1")]
        fz = sem("final_z_step")
        b_in = sem("layer_b_in")
        hw_in = [sem("head_weights_in0"), sem("head_weights_in1")]
        head_ps = sem("head_ps")
        row_max = sem("row_max")
        hr_a = sem("head_rope_shuffled")
        hr_b = sem("head_rope_cos")
        hr_c = sem("head_rope_sin")
        k_rot_step = sem("k_rot_step")
        k_rot_done = sem("k_rot_done")
        rms_std = sem("rms_std")
        rms_r = sem("rms_r")
        lat_scaled = sem("lat_scaled")
        lat_ps = sem("lat_ps")
        lat_t = sem("lat_t")
        head_act = sem("head_act")
        head_dve = sem("head_dve")
        out_stored = sem("out_stored")
        ov = [{n: sem(f"ov{l}_{n}") for n in
               ("w_in", "gi", "si", "xs", "xst", "xsto", "gate", "up", "silu", "h", "down", "y", "out")}
              for l in range(DEPTH)]

        block = ctx.enter_context(nc.Block())

        def fence(eng):
            eng.sem_inc(fenced[eng.engine], 1)

        LAYER_UNITS = [NG * TT + TT, MLA_H * TT + TT]
        unit0 = {(0, g): g * TT for g in range(NG)}
        unit0[(0, "mem")] = NG * TT
        unit0[(1, "mla")] = LAYER_UNITS[0]
        unit0[(1, "mem")] = LAYER_UNITS[0] + MLA_H * TT
        staged0 = {(0, g): g * TT for g in range(NG)}
        staged0[(0, "mem")] = NG * TT
        staged0[(1, "mem")] = NG * TT + TT
        DEN0 = {0: 0, "mla": TT, 1: TT + MLA_H * TT}

        def window(g, v):
            i, c = v
            if g == "mem":
                return 0, 0, 2
            if g == 0:
                return (2 * i + c) * P, 2 * i + c, 2
            if g == 1:
                return DH + (i + c // 2) * 256, (i + c // 2) * 2, 2
            return DH + (2 * i + c) * P, 2 * i + c, 1

        def pipeline(eng, step):
            step((0, -1), True, False, False)
            step((0, 0), True, True, False)
            step((0, 1), True, True, True)
            step((0, 2), True, True, True)
            with eng.Fori(1, (TT - 2) // 2) as i:
                step((i, 1), True, True, True)
                step((i, 2), True, True, True)
            step((0, TT - 1), False, True, True)
            step((0, TT), False, False, True)

        def plus(v, k):
            return (v[0], v[1] + k)

        def idx(v):
            return 2 * v[0] + v[1]

        def early(v, n):
            return isinstance(v[0], int) and idx(v) < n

        STORED0, STORED_PER, STORED_ALL = (0, 64, 128), (16, 16, 32), 256

        def latent_idx(v):
            return 2 * TT * v[0] + v[1]

        def projects(v):
            last_head = isinstance(v[0], int) and latent_idx(v) >= (MLA_H - 1) * TT
            return 2 <= v[1] % TT < 6 and not last_head

        def latent_pipeline(eng, step):
            step((0, -1), True, False, False)
            step((0, 0), True, True, False)
            with eng.Fori(0, MLA_H // 2 - 1) as i:
                for c in range(1, 2 * TT + 1):
                    step((i, c), True, True, True)
            i = MLA_H // 2 - 1
            for c in range(1, 2 * TT + 1):
                step((i, c), c < 2 * TT - 1, c < 2 * TT, True)

        def kv_of(layer, g):
            return (km_t, v_mem, qm_t) if g == "mem" else (k_t, v_a, q_t)

        def proj_counts():
            c, a, d = {}, 0, 0
            for g in range(NG):
                c[("A", g)] = (a, d)
                a += (9 if g == 0 else 8) + (4 if g == 0 else 0)
                d += 8
            c["B"] = (a, d)
            return c
        PC = proj_counts()
        W_PARTS = ("exp_w_gate", "exp_w_up", "exp_w_down")

        def part_slot(e_par, m):
            return (3 * e_par + m + 2) % 6

        def part_view(slot, m):
            return ring_at(16 * slot, KT, DE) if m < 2 else ring_at(16 * slot, 4, D)

        def part_src(l, m, e):
            w = io[W_PARTS[m]][l, bass.ds(e, 1)]
            return w.rearrange("a (k p) n -> p (a k) n", p=P)

        RING_USES = NE // 2


        MEMQ_DONE = [PC[("A", 0)][0] + 13, PC["B"][0] + 12]

        N_TABLE = N_GRP + NE + NE + NE * NE + NCHUNK + NOVER
        ROUTE_TABLE = at(72, N_TABLE)
        T_TIEG = ROUTE_TABLE[:, 0:N_GRP]
        o0 = N_GRP
        T_TIEE = ROUTE_TABLE[:, o0:o0 + NE]
        o0 += NE
        T_BASE = ROUTE_TABLE[:, o0:o0 + NE]
        o0 += NE
        T_TRI = ROUTE_TABLE[:, o0:o0 + NE * NE].rearrange("p (a b) -> p a b", b=NE)
        o0 += NE * NE
        T_THR = ROUTE_TABLE[:, o0:o0 + NCHUNK]
        o0 += NCHUNK
        T_CHUNK = ROUTE_TABLE[:, o0:o0 + NOVER]
        rt = [at(64 + i, TT, NE) for i in range(8)]
        hot_g = at(78, TT, N_GRP)
        r_one = at(76.5, 7, TT)
        r_eg = at(77, TT, N_GRP)
        r_exp = at(77.25, 2, NE)
        r_chunk = at(77.5, NOVER + 1)
        r_slot = at(77.75, 2, TT)
        hot_both = at(80, TT, NE)
        counts = at(81, NE)
        big_tmp = at(82, NE, NE)
        rank = at(86, TT, NE)

        @block.sync
        def _(sp):
            def mem_loads(l):
                w = io["mem_w_kv"][l].rearrange("(k p) n -> p k n", p=P)
                sp.dma_start(mem_w[l], w).then_inc(mem_in, 16)
                sp.dma_start(mem_t[l], io["mem_t"].rearrange("(k p) n -> p k n", p=P)).then_inc(mem_in, 16)

            def group_loads(g):
                b = g % 2
                if g == 1:
                    sp.wait_ge(mem_proj, 1)
                if g == 2:
                    sp.wait_ge(dve_full, 8)
                    sp.wait_ge(act_full, 13)
                w = io["a_w_in"][0].rearrange("(k p) n -> p k n", p=P)
                for j in (2, 0, 1):
                    sp.dma_start(w_a[b][:, j], w[:, :, j * NG * GW + g * GW:j * NG * GW + (g + 1) * GW]).then_inc(w_in[b], 16)
                for h in range(4):
                    sp.dma_start(x_t[b][:, 2 * h:2 * h + 2], io["x_t"][g].rearrange("(k p) n -> p k n", p=P)[:, 2 * h:2 * h + 2]).then_inc(x_in[b], 16)
                if g == 0:
                    sp.wait_ge(mem_proj, 1)
                    sp.dma_start(w_qm_a, w[:, :, 3 * NG * GW:]).then_inc(wqm_in, 16)

            def rope_loads(g):
                if g > 0:
                    sp.wait_ge(probs_t, g * TT)
                sp.dma_start(rope_a, io["rope_a"][g].rearrange("c p n -> p c n")).then_inc(rope_in, 16)

            def mask_load(g, v):
                u = unit0[(0, g)] + idx(v)
                b = v[1] % 2
                if g > 0 or not early(v, 2):
                    sp.wait_ge(masked, u - 1)
                fence(sp)
                sp.dma_start(masked_by[:, b], io["masks"][g, bass.ds(idx(v), 1)].rearrange("a p n -> p (a n)")).then_inc(mask_in[b], 16)

            mem_loads(0)
            sp.dma_start(ident[:], io["ident"]).then_inc(consts_in, 16)
            sp.dma_start(tri[:], io["tri"]).then_inc(consts_in, 16)
            sp.dma_start(infos[:], io["infos"]).then_inc(infos_in, 16)
            group_loads(0)
            rope_loads(0)
            for l in range(DEPTH):
                sp.dma_start(slot_d[l], io["nowhere"]).then_inc(slots_cleared, 16)
            group_loads(1)
            for g in range(NG):
                mask_load(g, (0, 0))
                mask_load(g, (0, 1))
                with sp.Fori(0, (TT - 2) // 2) as i:
                    mask_load(g, (i, 2))
                    mask_load(g, (i, 3))
                if g + 1 < NG:
                    rope_loads(g + 1)
                if g == 0:
                    group_loads(2)
            sp.wait_ge(act_full, PC["B"][0])
            sp.wait_ge(dve_full, PC["B"][1])
            sp.dma_start(X, io["x"].rearrange("(t p) d -> p t d", p=P)).then_inc(x_res_in, 16)
            sp.dma_start(w_out[0], io["a_w_out"][0].rearrange("(k p) n -> p k n", p=P)).then_inc(wout_in, 16)

            def gb_loads(i, names, l):
                if i > 0:
                    sp.wait_ge(x_ready, i * TT)
                for c, n in enumerate(names):
                    sp.dma_start(ln_gb[:, c], io[n][l:l + 1].to_broadcast([P, D])).then_inc(gb_in, 16)

            def router_loads(l):
                if l > 0:
                    sp.wait_ge(r_ps, TT * l)
                    sp.wait_ge(r_out, TT * l)
                sp.dma_start(w_router[:, :, 0:N_GRP], io["router_w_grp"][l].rearrange("(k p) n -> p k n", p=P)).then_inc(router_in, 16)
                sp.dma_start(w_router[:, :, N_GRP:], io["router_w_exp"][l].rearrange("(k p) n -> p k n", p=P)).then_inc(router_in, 16)
                sp.dma_start(b_router[:, 0:N_GRP], io["router_b_grp"][l:l + 1].to_broadcast([P, N_GRP])).then_inc(router_in, 16)
                sp.dma_start(b_router[:, N_GRP:], io["router_b_exp"][l:l + 1].to_broadcast([P, NE])).then_inc(router_in, 16)

            gb_loads(0, ("ln_mix_g", "ln_mix_b"), 0)
            router_loads(0)
            for b in range(2):
                sp.wait_ge(o_stored[b], STORED_ALL)
            sp.wait_ge(scores, unit0[(0, "mem")])
            sp.wait_ge(pv, unit0[(0, "mem")])
            for g in range(NG):
                sp.dma_start(merged[:, :, g], og[g].rearrange("(t p) c -> p t c", p=P)).then_inc(merge_in, 16)

            def gather_idx(l, e, b, n):
                if not (isinstance(n, int) and n == 0):
                    sp.wait_ge(xs_in[b], 16 * n)
                fence(sp)
                sp.dma_start(g_idx[0:CAP, b], slot_d[l][bass.ds(e * CAP, CAP)]).then_inc(gi_in[b], 16)

            def scatter_idx(l, e, b, n):
                if not (isinstance(n, int) and n == 0):
                    sp.wait_ge(ys_out[b], 16 * n)
                fence(sp)
                sp.dma_start(s_idx[0:CAP, b], slot_d[l][bass.ds(e * CAP, CAP)]).then_inc(si_in[b], 16)

            def expert_phase(l):
                def part(e, b, m):
                    slot = part_slot(b, m)
                    fence(sp)
                    sp.dma_start(part_view(slot, m), part_src(l, m, e)).then_inc(ring_in[slot], 16)

                if l == 1:
                    sp.wait_ge(pv, unit0[(1, "mem")])
                part(0, 0, 0)
                part(0, 0, 1)
                sp.wait_ge(y_ps, TT * (l + 1))
                sp.dma_start(ROUTE_TABLE, io["route_table"].to_broadcast([P, N_TABLE])).then_inc(table_in, 16)
                part(0, 0, 2)
                for m in range(3):
                    part(1, 1, m)
                sp.wait_ge(slots_sent, 256 * (l + 1))
                for e in range(2):
                    gather_idx(l, e, e, RING_USES * l)
                    scatter_idx(l, e, e, RING_USES * l)
                gb_loads(1 + 2 * l, ("ln_ffn_g", "ln_ffn_b"), l)
                with sp.Fori(0, NE // 2 - 1) as i:
                    for b in range(2):
                        e = 2 * i + 2 + b
                        for m, used in enumerate((gate_ps, up_ps, down_ps)):
                            sp.wait_ge(used, NE * l + e - 1)
                            part(e, b, m)
                            if m == 0:
                                gather_idx(l, e, b, i + RING_USES * l + 1)
                        scatter_idx(l, e, b, i + RING_USES * l + 1)

                o = ov[l]
                sp.wait_ge(route_done, l + 1)
                sp.wait_ge(down_ps, NE * (l + 1))
                for b in range(2):
                    sp.wait_ge(ys_out[b], 256 * (l + 1))
                n_over = sp.value_load(over_i[0:1, NOVER:NOVER + 1], min_val=0, max_val=NOVER)
                with sp.If(n_over > 0):
                    with sp.Fori(0, n_over) as j:
                        e = sp.value_load(over_i[0:1, bass.ds(j, 1)], min_val=0, max_val=NE - 1)
                        for m in range(3):
                            sp.dma_start(part_view(m, m), part_src(l, m, e)).then_inc(o["w_in"], 16)
                        src = slot_d[l][bass.ds(j * CAP + NE * CAP, CAP)]
                        sp.dma_start(g_idx[0:CAP, 0], src).then_inc(o["gi"], 16)
                        sp.dma_start(s_idx[0:CAP, 0], src).then_inc(o["si"], 16)
                        sp.wait_ge(o["out"], 16 * j + 16)
                        fence(sp)
                with sp.Else():
                    sp.nop()
                sp.nop()

            def final_loads(l):
                for t in range(TT):
                    b = t % 2
                    if t >= 2:
                        sp.wait_ge(z_done, TT * (2 * l + 1) + t - 1)
                    for k in range(2):
                        sp.dma_start(y_in[:, b, k], y_d[l][k * S + t * P:k * S + (t + 1) * P]).then_inc(yin[b], 16)

            expert_phase(0)
            final_loads(0)
            w_b = io["b_w_in"][0].rearrange("(k p) n -> p k n", p=P)
            sp.dma_start(w_in_b, w_b).then_inc(b_in, 16)
            mem_loads(1)
            sp.dma_start(w_v, io["b_w_kvb"][0].rearrange("p (h c) -> p h c", c=2 * DH)[:, :, DH:]).then_inc(b_in, 16)
            sp.dma_start(w_out[1], io["b_w_out"][0].rearrange("(k p) n -> p k n", p=P)).then_inc(wout_in, 16)
            sp.dma_start(rope_b[DH:QKB], io["rope_b"].rearrange("c p n -> p c n")).then_inc(b_in, 16)
            sp.dma_start(rms_g[:], io["b_norms"]).then_inc(b_in, 16)

            def head_weights(h, hb, first):
                if not first:
                    sp.wait_ge(head_ps, 4 * h - 4)
                fence(sp)
                sp.dma_start(w_q_head[:, hb], io["b_w_qb"][0].rearrange("(k p) n -> p k n", p=P)[:, :, bass.ds(h * QKB, QKB)]).then_inc(hw_in[hb], 16)
                sp.dma_start(w_k_head[:, hb], io["b_w_kvb"][0][:, bass.ds(h * 2 * DH, DH)]).then_inc(hw_in[hb], 16)

            head_weights(0, 0, True)
            head_weights(1, 1, True)
            gb_loads(2, ("ln_mix_g", "ln_mix_b"), 1)
            router_loads(1)
            with sp.Fori(0, MLA_H // 2 - 1) as i:
                head_weights(2 * i + 2, 0, False)
                head_weights(2 * i + 3, 1, False)
            expert_phase(1)
            final_loads(1)
            for t in range(TT):
                sp.wait_ge(x_ready, 3 * TT + t + 1)
                sp.dma_start(io["out"][t * P:(t + 1) * P], X[:, t]).then_inc(out_stored, 16)
            sp.wait_ge(out_stored, 16 * TT)

        @block.gpsimd
        def _(pool):
            nc.gpsimd.memset(q_stage[:], 0.0).then_inc(zeroed, 1)
            nc.gpsimd.memset(ones[:], 1.0).then_inc(zeroed, 1)
            for c in (0, DH + S):
                last = nc.gpsimd.memset(k_t[:, :, c:c + DH], 0.0)
            last.then_inc(zeroed, 1)
            nc.gpsimd.memset(eps[:, 0:1], LN_EPS).then_inc(zeroed, 1)
            nc.gpsimd.memset(eps[:, 1:2], RMS_EPS).then_inc(zeroed, 1)
            pool.wait_ge(zeroed, 5)

            def stage(layer, g, v, free=True):
                q = kv_of(layer, g)[2]
                b = v[1] % 2
                if free:
                    pool.wait_ge(scores, unit0[(layer, g)] + idx(v) - 1)
                fence(pool)
                for hp in range(2):
                    last = nc.gpsimd.tensor_copy(q_stage[64 * hp:64 * hp + 64, b, hp::2, :],
                                                 q[64 * hp:64 * hp + 64, :, bass.ds(idx(v) * P, P)])
                last.then_inc(q_staged, 1)

            def store(g, v):
                u = idx(v)
                b = v[1] % 2
                pool.wait_ge(o_out, unit0[(0, g)] + u + 1)
                fence(pool)
                if g == 0:
                    pool.dma_start(og[g][bass.ds(u * P, P)], o_stage[:, b]).then_inc(o_stored[b], 16)
                elif g == 1:
                    rows = og[g].rearrange("(m r) c -> r m c", r=4)[bass.ds(v[0] + v[1] // 2, 1), P * b:P * b + P]
                    pool.dma_start(rows.rearrange("a m c -> (a m) c"), o_stage[:, b]).then_inc(o_stored[b], 16)
                else:
                    rows = og[g].rearrange("(m r) c -> r m c", r=16)
                    for rr in range(2):
                        pool.dma_start(rows[bass.ds(2 * u + rr, 1)].rearrange("a m c -> (a m) c"),
                                       o_stage[64 * rr:64 * rr + 64, b]).then_inc(o_stored[b], 16)

            for g in range(NG):
                pool.wait_ge(dve_free, 8 * (g + 1))
                stage(0, g, (0, 0), free=g > 0)
                stage(0, g, (0, 1), free=g > 0)
                with pool.Fori(0, (TT - 2) // 2) as i:
                    for c in range(2):
                        stage(0, g, (i, 2 + c))
                        store(g, (i, c))
                store(g, (0, TT - 2))
                store(g, (0, TT - 1))

            def stage_all(layer):
                pool.wait_ge(act_free, MEMQ_DONE[layer])
                stage(layer, "mem", (0, 0))
                stage(layer, "mem", (0, 1))
                with pool.Fori(0, (TT - 2) // 2) as i:
                    stage(layer, "mem", (i, 2))
                    stage(layer, "mem", (i, 3))

            def norm_scale(i, store_to=None):
                pool.wait_ge(gb_in, 32 * (i + 1))
                for t in range(TT):
                    n = i * TT + t + 1
                    pool.wait_ge(norm_done, n)
                    nc.gpsimd.tensor_tensor(X[:, t], X[:, t], ln_gb[:, 0], ALU.mult).then_inc(gmul_done, 1)
                    pool.wait_ge(gmul_done, n)
                    nc.gpsimd.tensor_tensor(X[:, t], X[:, t], ln_gb[:, 1], ALU.add).then_inc(x_ready, 1)
                    if store_to is not None:
                        pool.wait_ge(x_ready, n)
                        pool.dma_start(store_to[t * P:(t + 1) * P], X[:, t]).then_inc(x1_stored, 16)

            def experts(l):
                pool.wait_ge(r_ps, TT * (l + 1))
                nc.gpsimd.memset(xs[:], 0.0).then_inc(zeroed, 1)
                pool.wait_ge(zeroed, 6 + l)
                pool.wait_ge(route_done, l + 1)
                pool.wait_ge(slots_cleared, 32)
                pool.wait_ge(infos_in, 16)
                for t in range(TT):
                    for k in range(2):
                        pool.indirect_dma_start(slot_d[l][:, :], bass.IndirectOffsetOnAxis(ap=slots_i[:, t, k:k + 1], axis=0),
                                                infos[:, t, k, :], None).then_inc(slots_sent, 16)
                pool.wait_ge(x1_stored, 16 * TT * (l + 1))

                def gather(n, b, first):
                    pool.wait_ge(gi_in[b], 16 * n + 16)
                    if not first:
                        pool.wait_ge(xst_ps, 2 * n + b - 1)
                    fence(pool)
                    pool.indirect_dma_start(xs[0:CAP, b], None, x1_d[l][:, :],
                                            bass.IndirectOffsetOnAxis(ap=g_idx[0:CAP, b, 0:1], axis=0),
                                            bounds_check=S - 1, oob_is_err=False).then_inc(xs_in[b], 16)

                def scatter(n, b):
                    pool.wait_ge(si_in[b], 16 * n + 16)
                    pool.wait_ge(y_act, 2 * n + b + 1)
                    pool.wait_ge(y_dve, 2 * n + b + 1)
                    fence(pool)
                    pool.indirect_dma_start(y_d[l][:, :], bass.IndirectOffsetOnAxis(ap=s_idx[0:CAP, b, 1:2], axis=0),
                                            ys[0:CAP, b], None, bounds_check=2 * S - 1, oob_is_err=False).then_inc(ys_out[b], 16)
                n0 = RING_USES * l
                gather(n0, 0, True)
                gather(n0, 1, True)
                with pool.Fori(0, NE // 2 - 1) as i:
                    for b in range(2):
                        gather(n0 + i + 1, b, False)
                        scatter(n0 + i, b)
                for b in range(2):
                    scatter(n0 + NE // 2 - 1, b)
                o = ov[l]
                n_over = pool.value_load(over_i[0:1, NOVER:NOVER + 1], min_val=0, max_val=NOVER)
                with pool.If(n_over > 0):
                    with pool.Fori(0, n_over) as j:
                        pool.wait_ge(o["gi"], 16 * j + 16)
                        fence(pool)
                        pool.indirect_dma_start(xs[0:CAP, 0], None, x1_d[l][:, :],
                                                bass.IndirectOffsetOnAxis(ap=g_idx[0:CAP, 0, 0:1], axis=0),
                                                bounds_check=S - 1, oob_is_err=False).then_inc(o["xs"], 16)
                        pool.wait_ge(o["si"], 16 * j + 16)
                        pool.wait_ge(o["y"], j + 1)
                        fence(pool)
                        pool.indirect_dma_start(y_d[l][:, :], bass.IndirectOffsetOnAxis(ap=s_idx[0:CAP, 0, 1:2], axis=0),
                                                ys[0:CAP, 0], None, bounds_check=2 * S - 1, oob_is_err=False).then_inc(o["out"], 16)
                with pool.Else():
                    pool.nop()
                pool.nop()

            stage_all(0)
            norm_scale(0, x1_d[0])
            experts(0)
            norm_scale(1)
            stage_all(1)
            norm_scale(2, x1_d[1])
            experts(1)
            norm_scale(3)

        @block.tensor
        def _(pe):
            def mm(out, lhsT, rhs, start=True, stop=True):
                return nc.tensor.matmul(out, lhsT, rhs, start=start, stop=stop)

            def mem_projection(l):
                pe.wait_ge(mem_in, 32 * (l + 1))
                for j in range(2):
                    for k in range(KT):
                        mm(ps[:, 6, j * MEM:(j + 1) * MEM], mem_w[l][:, k, j * P:(j + 1) * P], mem_t[l][:, k], k == 0, k == KT - 1)
                for j in range(2):
                    for k in range(KT):
                        last = mm(ps[:, 7, j * GW:(j + 1) * GW], mem_t[l][:, k, j * P:(j + 1) * P], mem_w[l][:, k, GW:], k == 0, k == KT - 1)
                last.then_inc(mem_proj, 1)

            na, nd = [0], [0]

            def for_act(cols, products, bank0=4, rows=P):
                n = na[0]
                if n >= 2:
                    pe.wait_ge(act_free, n - 1)
                for k, (l_, r_) in enumerate(products):
                    last = mm(ps[0:rows, bank0 + n % 2, 0:cols], l_, r_, k == 0, k == len(products) - 1)
                last.then_inc(act_full, 1)
                na[0] += 1

            def for_dve(products):
                n = nd[0]
                if n >= 4:
                    pe.wait_ge(dve_free, n - 3)
                for k, (l_, r_) in enumerate(products):
                    last = mm(ps[:, n % 4, :], l_, r_, k == 0, k == KT - 1)
                last.then_inc(dve_full, 1)
                nd[0] += 1

            def group_projection(g):
                b = g % 2
                uses = g // 2 + 1
                pe.wait_ge(w_in[b], 48 * uses)
                pe.wait_ge(x_in[b], 64 * uses)
                if g > 0:
                    pe.wait_ge(o_out, g * TT)
                for t in range(9 if g == 0 else 8):
                    c0 = t * P + (0 if g == 0 else DH)
                    for_act(GW, [(x_t[b][:, k, c0:c0 + P], w_a[b][:, 2, k]) for k in range(KT)])
                for j in range(4):
                    for h in range(2):
                        c0 = DH + h * HALF
                        for_dve([(w_a[b][:, j // 2, k, (j % 2) * P:(j % 2 + 1) * P], x_t[b][:, k, c0:c0 + HALF]) for k in range(KT)])
                if g == 0:
                    pe.wait_ge(wqm_in, 16)
                    for j in range(2):
                        for h in range(2):
                            c0 = DH + h * HALF
                            for_act(HALF, [(w_qm_a[:, k, j * P:(j + 1) * P], x_t[b][:, k, c0:c0 + HALF]) for k in range(KT)])

            def group_attention(layer, g):
                keys, vals, _ = kv_of(layer, g)
                u0 = unit0[(layer, g)]

                def step(v, ahead, now, behind):
                    if ahead:
                        w = plus(v, 1)
                        b = w[1] % 2
                        col, _, nch = window(g, w)
                        pe.wait_ge(q_staged, staged0[(layer, g)] + idx(w) + 1)
                        if u0 > 0 or not early(w, 2):
                            pe.wait_ge(probs, u0 + idx(w) - 1)
                        for h in range(GH):
                            last = mm(ps[:, 2 * b + h // 2, (h % 2) * 256:(h % 2) * 256 + nch * P], q_stage[:, b, h],
                                      keys[:, h // 2, bass.ds(col, nch * P)])
                        last.then_inc(scores, 1)
                    if now:
                        b = v[1] % 2
                        _, _, nch = window(g, v)
                        u = u0 + idx(v)
                        pe.wait_ge(probs, u + 1)
                        if u0 > 0 or not early(v, 1):
                            pe.wait_ge(pt_act, u)
                            pe.wait_ge(pt_dve, u)
                        for h in range(GH):
                            for c in range(nch):
                                last = nc.tensor.transpose(ps[:, 4 + h // 2, (h % 2) * 256 + c * P:(h % 2) * 256 + (c + 1) * P],
                                                           prob[:, b, h * 256 + c * P:h * 256 + (c + 1) * P], ident[:])
                        last.then_inc(probs_t, 1)
                    if behind:
                        w = plus(v, -1)
                        b = w[1] % 2
                        _, vt, nch = window(g, w)
                        u = u0 + idx(w)
                        pe.wait_ge(pt_act, u + 1)
                        pe.wait_ge(pt_dve, u + 1)
                        if u0 > 0 or not early(w, 2):
                            pe.wait_ge(o_out, u - 1)
                        for h in range(GH):
                            for c in range(nch):
                                last = mm(ps[:, 6 + b, h * DH:(h + 1) * DH], prob_t[:, b, h * 256 + c * P:h * 256 + (c + 1) * P],
                                          vals[:, bass.ds(vt + c, 1), h * DH:(h + 1) * DH].rearrange("p a n -> p (a n)"), c == 0, c == nch - 1)
                        last.then_inc(pv, 1)
                if layer == 0 and g != "mem":
                    pe.wait_ge(act_free, PC[("A", g)][0] + (9 if g == 0 else 8))
                    pe.wait_ge(dve_free, 8 * (g + 1))
                else:
                    pe.wait_ge(mem_kv_act, layer + 1)
                    pe.wait_ge(mem_kv_dve, layer + 1)
                pipeline(pe, step)

            def out_projection(l):
                nct = 4 if l == 0 else 6
                pe.wait_ge(o_out, unit0[(l, "mem")] + TT)
                pe.wait_ge(mix_done, 1)
                pe.wait_ge(wout_in, 16 * (l + 1))
                pe.wait_ge(router_in, 64 * (l + 1))
                n0 = l * TT

                def mix_transposes(t):
                    n = n0 + t
                    if n > 0:
                        pe.wait_ge(mixt_act, n)
                    if t > 3:
                        pe.wait_ge(r_out, n - 3)
                    for c in range(nct):
                        last = nc.tensor.transpose(ps[:, 4 + c // 4, (c % 4) * P:(c % 4 + 1) * P], mix[l][:, t, c * P:(c + 1) * P], ident[:])
                    last.then_inc(mixt_ps, 1)

                def products(t):
                    n = n0 + t
                    pe.wait_ge(mixt_act, n + 1)
                    b = t % 2
                    if n >= 2:
                        pe.wait_ge(z_done, 2 * l * TT + t - 1)
                    for h in range(2):
                        for c in range(nct):
                            last = mm(ps[:, 2 * b + h], mix_t[:, b, c], w_out[l][:, c, h * HALF:(h + 1) * HALF], c == 0, c == nct - 1)
                    last.then_inc(y_ps, 1)

                mix_transposes(0)
                for t in range(TT + 2):
                    if t + 1 < TT:
                        mix_transposes(t + 1)
                    if t < TT:
                        products(t)
                    if t >= 2:
                        token_transposes(2 * l, t - 2)
                        router(l, t - 2)

            def token_transposes(i, t):
                n = i * TT + t
                pe.wait_ge(x_ready, n + 1)
                if t == 0 and i == 0:
                    pe.wait_ge(o_out, LAYER_UNITS[0])
                if n > 0:
                    pe.wait_ge(xt_act, n)
                    pe.wait_ge(xt_dve, n)
                for k in range(KT):
                    last = nc.tensor.transpose(ps[:, 6 + k // 4, (k % 4) * P:(k % 4 + 1) * P], X[:, t, k * P:(k + 1) * P], ident[:])
                last.then_inc(xt_ps, 1)

            def router(l, t):
                pe.wait_ge(xt_act, 2 * l * TT + t + 1)
                pe.wait_ge(xt_dve, 2 * l * TT + t + 1)
                if l * TT + t > 0:
                    pe.wait_ge(r_out, l * TT + t)
                pe.wait_ge(mixt_act, l * TT + min(t + 4, TT))
                for k in range(KT):
                    last = mm(ps[:, 5, 256:256 + NR], XT[:, k, t * P:(t + 1) * P], w_router[:, k], k == 0, k == KT - 1)
                last.then_inc(r_ps, 1)

            def ranks(l):
                pe.wait_ge(route_hot, l + 1)
                for t in range(TT):
                    for i in range(t + 1):
                        mm(ps[:, 0, t * NE:(t + 1) * NE], tri[:] if i == t else ones[:], hot_both[:, i], i == 0, i == t)
                for i in range(TT):
                    last = mm(ps[:, 1, 0:NE], ones[:], hot_both[:, i], i == 0, i == TT - 1)
                last.then_inc(rank_ps, 1)

            def row_transposes(b):
                for k in range(KT):
                    last = nc.tensor.transpose(ps[:, k // 4, (k % 4) * CAP:(k % 4 + 1) * CAP], xs[0:CAP, b, k * P:(k + 1) * P], ident[0:CAP, 0:CAP])
                return last

            def hidden(bank, w, b):
                for f in range(4):
                    for k in range(KT):
                        last = mm(ps[:, bank, f * CAP:(f + 1) * CAP], w[:, k, f * P:(f + 1) * P], xs_t[b][:, k], k == 0, k == KT - 1)
                return last

            def down(w, b):
                for h in range(2):
                    for f in range(4):
                        last = mm(ps[0:CAP, 4 + 2 * b + h, :], h_t[b][:, f], w[:, f, h * HALF:(h + 1) * HALF], f == 0, f == 3)
                return last

            def experts(l):
                n0 = NE * l
                r0 = RING_USES * l

                def rows(e, n, b):
                    pe.wait_ge(xs_in[b], 16 * n + 16)
                    if not (isinstance(e, int) and e == 0):
                        pe.wait_ge(xst_out, n0 + e)
                    row_transposes(b).then_inc(xst_ps, 1)

                def expert(e, n, b, more, first=False):
                    pe.wait_ge(ring_in[part_slot(b, 0)], 16 * n + 16)
                    pe.wait_ge(xst_out, n0 + e + 1)
                    if not first:
                        pe.wait_ge(silu_done, n0 + e)
                    hidden(2, part_view(part_slot(b, 0), 0), b).then_inc(gate_ps, 1)
                    pe.wait_ge(ring_in[part_slot(b, 1)], 16 * n + 16)
                    if not first:
                        pe.wait_ge(h_done, n0 + e)
                    hidden(3, part_view(part_slot(b, 1), 1), b).then_inc(up_ps, 1)
                    if more:
                        rows(e + 1, n + b, 1 - b)
                    pe.wait_ge(ring_in[part_slot(b, 2)], 16 * n + 16)
                    pe.wait_ge(h_done, n0 + e + 1)
                    if not (isinstance(e, int) and n0 + e < 2):
                        pe.wait_ge(y_act, n0 + e - 1)
                        pe.wait_ge(y_dve, n0 + e - 1)
                    down(part_view(part_slot(b, 2), 2), b).then_inc(down_ps, 1)

                pe.wait_ge(route_done, l + 1)
                rows(0, r0, 0)
                expert(0, r0, 0, True, first=l == 0)
                expert(1, r0, 1, True)
                with pe.Fori(0, NE // 2 - 2) as i:
                    expert(2 * i + 2, r0 + i + 1, 0, True)
                    expert(2 * i + 3, r0 + i + 1, 1, True)
                expert(NE - 2, r0 + NE // 2 - 1, 0, True)
                expert(NE - 1, r0 + NE // 2 - 1, 1, False)
                o = ov[l]
                pe.wait_ge(y_act, n0 + NE)
                pe.wait_ge(y_dve, n0 + NE)
                n_over = pe.value_load(over_i[0:1, NOVER:NOVER + 1], min_val=0, max_val=NOVER)
                with pe.If(n_over > 0):
                    with pe.Fori(0, n_over) as j:
                        pe.wait_ge(o["xs"], 16 * j + 16)
                        row_transposes(0).then_inc(o["xst"], 1)
                        pe.wait_ge(o["w_in"], 48 * j + 48)
                        pe.wait_ge(o["xsto"], j + 1)
                        hidden(2, part_view(0, 0), 0).then_inc(o["gate"], 1)
                        hidden(3, part_view(1, 1), 0).then_inc(o["up"], 1)
                        pe.wait_ge(o["h"], j + 1)
                        down(part_view(2, 2), 0).then_inc(o["down"], 1)
                with pe.Else():
                    pe.nop()
                pe.nop()

            def latent_projection():
                pe.wait_ge(b_in, 64)
                pe.wait_ge(xt_act, 2 * TT)
                pe.wait_ge(xt_dve, 2 * TT)
                for t in range(TT):
                    for_act(LAT, [(XT[:, k, t * P:(t + 1) * P], w_in_b[:, k, 0:LAT]) for k in range(KT)])
                for j in range(2):
                    for h in range(2):
                        for_act(HALF, [(w_in_b[:, k, LAT + j * P:LAT + (j + 1) * P], XT[:, k, h * HALF:(h + 1) * HALF]) for k in range(KT)])
                mem_projection(1)
                for t in range(TT):
                    pe.wait_ge(lat_scaled, t + 1)
                    if t >= 2:
                        pe.wait_ge(lat_t, t - 1)
                    bank = 2 * (t % 2)
                    for c in range(3):
                        nc.tensor.transpose(ps[:, bank, c * P:(c + 1) * P], latent[:, t, c * P:(c + 1) * P], ident[:])
                    nc.tensor.transpose(ps[0:QKB, bank + 1, 0:P], latent[:, t, LAT - QKB:LAT], ident[:]).then_inc(lat_ps, 1)
                pe.wait_ge(lat_t, TT)
                for t in range(TT):
                    for_act(HALF, [(ckv_t[:, t * P:(t + 1) * P], w_v.rearrange("p h c -> p (h c)"))])

            def head_projection(h, hb, j):
                if j == 0:
                    pe.wait_ge(hw_in[hb], 16 * h + 32 - 16 * hb)
                if not (isinstance(h, int) and h == 0 and j == 0):
                    pe.wait_ge(head_act, 4 * h + j)
                    pe.wait_ge(head_dve, 2 * h + min(j, 2))
                cols = slice((j % 2) * HALF, (j % 2 + 1) * HALF)
                if j < 2:
                    for k in range(2):
                        last = mm(ps[0:QKB, 7, :], w_q_head[:, hb, k], cq_t[:, k, cols], k == 0, k == 1)
                else:
                    last = mm(ps[0:DH, 7, :], w_k_head[:, hb], ckv_t[:, cols])
                last.then_inc(head_ps, 1)

            def latent_attention():
                u0 = unit0[(1, "mla")]
                pe.wait_ge(act_free, PC["B"][0] + 20)
                pe.wait_ge(k_rot_done, 1)
                for j in range(4):
                    head_projection(0, 0, j)

                def step(v, ahead, now, behind):
                    if ahead:
                        w = plus(v, 1)
                        n, b, t = latent_idx(w), w[1] % 2, w[1] % TT
                        h, hb = 2 * w[0] + w[1] // TT, (w[1] // TT) % 2
                        if t == 0:
                            pe.wait_ge(head_act, 4 * h + 4)
                            pe.wait_ge(head_dve, 2 * h + 2)
                        pe.wait_ge(probs, u0 + n - 1)
                        for c in range(2):
                            last = mm(ps[:, 2 * b + c], q_head[0:QKB, hb, t * P:(t + 1) * P], k_head[0:QKB, hb, c * HALF:(c + 1) * HALF])
                        last.then_inc(scores, 1)
                    if now:
                        n, b, t = latent_idx(v), v[1] % 2, v[1] % TT
                        pe.wait_ge(probs, u0 + n + 1)
                        pe.wait_ge(pt_act, u0 + n)
                        pe.wait_ge(pt_dve, u0 + n)
                        for c in range(TT):
                            last = nc.tensor.transpose(ps[:, 4 + c // 4, (c % 4) * P:(c % 4 + 1) * P], prob[:, b, c * P:(c + 1) * P], ident[:])
                        last.then_inc(probs_t, 1)
                        if projects(v):
                            head_projection(2 * v[0] + v[1] // TT + 1, (v[1] // TT + 1) % 2, t - 2)
                    if behind:
                        w = plus(v, -1)
                        n, b = latent_idx(w), w[1] % 2
                        h = 2 * w[0] + w[1] // TT
                        pe.wait_ge(pt_act, u0 + n + 1)
                        pe.wait_ge(pt_dve, u0 + n + 1)
                        pe.wait_ge(o_out, u0 + n)
                        for c in range(TT):
                            last = mm(ps[:, 6, b * DH:(b + 1) * DH], prob_t[:, b, c * P:(c + 1) * P], v_b[:, c, bass.ds(h * DH, DH)], c == 0, c == TT - 1)
                        last.then_inc(pv, 1)
                latent_pipeline(pe, step)

            pe.wait_ge(consts_in, 32)
            pe.wait_ge(zeroed, 5)
            mem_projection(0)
            for g in range(NG):
                group_projection(g)
                group_attention(0, g)
            group_attention(0, "mem")
            out_projection(0)
            ranks(0)
            experts(0)
            for t in range(TT):
                token_transposes(1, t)
            latent_projection()
            latent_attention()
            group_attention(1, "mem")
            out_projection(1)
            ranks(1)
            experts(1)

        @block.scalar
        def _(act):
            na = [0]

            def copy_out(dst, rows=P):
                n = na[0]
                act.wait_ge(act_full, n + 1)
                cols = 1
                src = ps[0:rows, 4 + n % 2, 0:dst.shape[-1]]
                nc.scalar.copy(dst, src).then_inc(act_free, 1)
                na[0] += 1

            def mem_keys(l):
                act.wait_ge(mem_proj, l + 1)
                nc.scalar.copy(km_t[:], ps[:, 6].rearrange("p (a b) -> p a b", a=2)).then_inc(mem_kv_act, 1)

            def group_values(g):
                if g > 0:
                    act.wait_ge(pv, g * TT)
                for t in range(9 if g == 0 else 8):
                    copy_out(v_a[:, t])
                if g == 0:
                    for j in range(2):
                        for h in range(2):
                            copy_out(qm_t[:, j, h * HALF:(h + 1) * HALF])

            def group_attention(layer, g):
                u0 = unit0[(layer, g)]
                nch = window(g, (0, 0))[2]
                w = nch * P

                def step(v, ahead, now, behind):
                    if ahead:
                        x = plus(v, 1)
                        b = x[1] % 2
                        u = u0 + idx(x)
                        act.wait_ge(max_ready, u + 1)
                        for h in range(GH):
                            p = prob[:, b, h * 256:h * 256 + w]
                            last = nc.scalar.activation(p, p, ACT.Exp, bias=neg_max[:, b, h:h + 1], scale=SCALE_A,
                                                        accum_out=stat[:, b, 1, h:h + 1])
                        last.then_inc(probs, 1)
                    if now:
                        u = u0 + idx(v)
                        b = v[1] % 2
                        act.wait_ge(probs_t, u + 1)
                        if g != "mem":
                            if not (g == 0 and early(v, 2)):
                                act.wait_ge(o_stored[b], STORED0[g] + STORED_PER[g] * (v[0] + v[1] // 2))
                            act.wait_ge(probs, u + 1)
                            nc.scalar.copy(o_stage[:, b, GW:], stat[:, b].rearrange("p a h -> p (a h)")).then_inc(stat_kept, 1)
                        if u0 > 0 or not early(v, 2):
                            act.wait_ge(pv, u - 1)
                        if nch == 2:
                            nc.scalar.copy(prob_t[:, b, 0:HALF], ps[:, 4]).then_inc(pt_act, 1)
                        else:
                            nc.scalar.copy(prob_t[:, b, 0:HALF].rearrange("p (a b) -> p a b", a=2)[:, :, 0:P],
                                           ps[:, 4].rearrange("p (a b) -> p a b", a=2)[:, :, 0:P]).then_inc(pt_act, 1)
                    if behind and g != "mem":
                        x = plus(v, -1)
                        b = x[1] % 2
                        act.wait_ge(pv, u0 + idx(x) + 1)
                        nc.scalar.copy(o_stage[:, b, 0:GW], ps[:, 6 + b, 0:GW]).then_inc(o_out, 1)
                pipeline(act, step)

            def merge_exps():
                act.wait_ge(merge_diff, 1)
                nc.scalar.activation(merge_e[:], merge_e[:], ACT.Exp, scale=SCALE_A).then_inc(merge_exp, 1)

            def std_and_norm(i, t):
                n = i * TT + t + 1
                act.wait_ge(mv_done, n)
                nc.scalar.activation(std[:, t:t + 1], mean_var[:, t, 1:2], ACT.Sqrt, bias=eps[:, 0:1]).then_inc(sd_done, 1)
                act.wait_ge(rs_done, n)
                nc.scalar.activation(X[:, t], X[:, t], ACT.Identity, bias=rstd[:, t, 1:2], scale=rstd[:, t, 0:1]).then_inc(norm_done, 1)

            def token_copies(i, t):
                n = i * TT + t + 1
                act.wait_ge(xt_ps, n)
                nc.scalar.copy(XT[:, 0:4, t * P:(t + 1) * P], ps[:, 6].rearrange("p (a b) -> p a b", a=4)).then_inc(xt_act, 1)

            def out_projection(l):
                nct = 4 if l == 0 else 6

                def mix_copy(t):
                    act.wait_ge(mixt_ps, l * TT + t + 1)
                    if l * TT + t >= 2:
                        act.wait_ge(y_ps, l * TT + t - 1)
                    src = ps[:, 4:6].rearrange("p a b -> p (a b)")[:, 0:nct * P]
                    nc.scalar.copy(mix_t[:, t % 2, 0:nct].rearrange("p a b -> p (a b)"), src).then_inc(mixt_act, 1)
                mix_copy(0)
                for t in range(TT + 2):
                    if t + 1 < TT:
                        mix_copy(t + 1)
                    if 1 <= t < TT + 1:
                        std_and_norm(2 * l, t - 1)
                    if t >= 2:
                        token_copies(2 * l, t - 2)

            def routing(l):
                act.wait_ge(route_exp_in, 2 * l + 1)
                nc.scalar.activation(r_eg[:], r_eg[:], ACT.Exp).then_inc(route_exp, 1)
                act.wait_ge(route_exp_in, 2 * l + 2)
                nc.scalar.activation(r_one[:, 5], r_one[:, 5], ACT.Exp).then_inc(route_exp, 1)

            def silu(b):
                return nc.scalar.activation(sil[b], ps[:, 2, 0:4 * CAP].rearrange("p (a b) -> p a b", a=4), ACT.Silu)

            def experts(l):
                n0 = NE * l
                r0 = RING_USES * l

                def expert(e, b, n):
                    act.wait_ge(gate_ps, n0 + e + 1)
                    silu(b).then_inc(silu_done, 1)
                    act.wait_ge(down_ps, n0 + e + 1)
                    if not (isinstance(n, int) and n == 0):
                        act.wait_ge(ys_out[b], 16 * n)
                    nc.scalar.copy(ys[0:CAP, b, 0:HALF], ps[0:CAP, 4 + 2 * b]).then_inc(y_act, 1)

                expert(0, 0, r0)
                expert(1, 1, r0)
                with act.Fori(0, NE // 2 - 2) as i:
                    expert(2 * i + 2, 0, r0 + i + 1)
                    expert(2 * i + 3, 1, r0 + i + 1)
                expert(NE - 2, 0, r0 + NE // 2 - 1)
                expert(NE - 1, 1, r0 + NE // 2 - 1)
                o = ov[l]
                act.wait_ge(route_done, l + 1)
                n_over = act.value_load(over_i[0:1, NOVER:NOVER + 1], min_val=0, max_val=NOVER)
                with act.If(n_over > 0):
                    with act.Fori(0, n_over) as j:
                        act.wait_ge(o["gate"], j + 1)
                        silu(0).then_inc(o["silu"], 1)
                with act.Else():
                    act.nop()
                act.nop()

            def latent_norms():
                for t in range(TT):
                    n = na[0]
                    act.wait_ge(act_full, n + 1)
                    bank = 4 + n % 2
                    if t >= 2:
                        act.wait_ge(act_free, n - 1)
                    for c, (lo, hi) in enumerate(((0, QL), (QL, QL + KVL))):
                        nc.scalar.activation(square[:, t % 2, lo:hi], ps[:, bank, lo:hi], ACT.Square, accum_out=rms_ss[:, t, c:c + 1])
                    nc.scalar.copy(latent[:, t], ps[:, bank, 0:LAT]).then_inc(act_free, 1)
                    na[0] += 1
                for j in range(2):
                    for h in range(2):
                        copy_out(qm_t[:, j, h * HALF:(h + 1) * HALF])
                act.wait_ge(act_free, PC["B"][0] + TT)
                for c, width in enumerate((QL, KVL)):
                    last = nc.scalar.activation(rms_ss[:, :, c], rms_ss[:, :, c], ACT.Sqrt, bias=eps[:, 1:2], scale=1.0 / width)
                last.then_inc(rms_std, 1)
                mem_keys(1)
                for t in range(TT):
                    act.wait_ge(lat_ps, t + 1)
                    bank = 2 * (t % 2)
                    for c in range(3):
                        dst = cq_t[:, c, t * P:(t + 1) * P] if c < 2 else ckv_t[:, t * P:(t + 1) * P]
                        nc.scalar.activation(dst, ps[:, bank, c * P:(c + 1) * P], ACT.Copy, scale=rms_g[:, c:c + 1])
                    nc.scalar.copy(k_rot[DH:QKB, t * P:(t + 1) * P], ps[DH:QKB, bank + 1, 0:P]).then_inc(lat_t, 1)
                for t in range(TT):
                    copy_out(v_b[:, t])

            def head_copy(h, hb, j):
                act.wait_ge(head_ps, 4 * h + j + 1)
                act.wait_ge(scores, unit0[(1, "mla")] - TT + TT * h)
                dst = (q_head if j < 2 else k_head)[0:DH, hb, (j % 2) * HALF:(j % 2 + 1) * HALF]
                nc.scalar.copy(dst, ps[0:DH, 7]).then_inc(head_act, 1)

            def latent_attention():
                u0 = unit0[(1, "mla")]
                for j in range(4):
                    head_copy(0, 0, j)

                def step(v, ahead, now, behind):
                    if ahead:
                        w = plus(v, 1)
                        n, b = latent_idx(w), w[1] % 2
                        act.wait_ge(max_ready, u0 + n + 1)
                        act.wait_ge(probs_t, u0 + n - 1)
                        nc.scalar.activation(prob[:, b], ps[:, 2 * b:2 * b + 2].rearrange("p a b -> p (a b)"), ACT.Exp,
                                             bias=neg_max[:, b, 0:1], scale=SCALE_B, accum_out=stat[:, b, 1, 0:1]).then_inc(probs, 1)
                    if now:
                        n, b = latent_idx(v), v[1] % 2
                        act.wait_ge(probs_t, u0 + n + 1)
                        act.wait_ge(pv, u0 + n - 1)
                        nc.scalar.copy(prob_t[:, b, 0:HALF], ps[:, 4]).then_inc(pt_act, 1)
                        if projects(v):
                            head_copy(2 * v[0] + v[1] // TT + 1, (v[1] // TT + 1) % 2, v[1] % TT - 2)
                latent_pipeline(act, step)

            act.wait_ge(zeroed, 5)
            mem_keys(0)
            for g in range(NG):
                group_values(g)
                group_attention(0, g)
            group_attention(0, "mem")
            merge_exps()
            out_projection(0)
            routing(0)
            experts(0)
            for t in range(TT + 1):
                if t < TT:
                    std_and_norm(1, t)
                if t >= 1:
                    token_copies(1, t - 1)
            latent_norms()
            latent_attention()
            group_attention(1, "mem")
            out_projection(1)
            routing(1)
            experts(1)
            for t in range(TT):
                std_and_norm(3, t)

        @block.vector
        def _(dve):
            def chain(s, count):
                def link(ins):
                    count[0] += 1
                    ins.then_inc(s, 1)
                    dve.wait_ge(s, count[0])
                return link

            merge_link = chain(mstep, [0])
            route_link = chain(rstep, [0])
            ln_link = chain(rs_step, [0])

            def mem_values(l):
                dve.wait_ge(mem_proj, l + 1)
                nc.vector.tensor_copy(v_mem[:], ps[:, 7].rearrange("p (a b) -> p a b", a=2)).then_inc(mem_kv_dve, 1)

            swap_a = [(i + 8) % 16 if i < 16 else i for i in range(32)]
            swap_b = [(i + 16) % 32 for i in range(32)]

            def group_rope(g):
                dve.wait_ge(rope_in, 16 * (g + 1))
                if g > 0:
                    dve.wait_ge(scores, g * TT)
                    dve.wait_ge(pv, g * TT)
                for j in range(4):
                    for h in range(2):
                        n = g * 8 + 2 * j + h
                        b = n % 2
                        bank = ps[:, n % 4]
                        cols = slice(h * HALF, (h + 1) * HALF)
                        dve.wait_ge(dve_full, n + 1)
                        nc.vector.stream_shuffle(rope_tmp[:, 2 * b], bank, swap_a).then_inc(rope_a_s, 1)
                        nc.vector.tensor_tensor(rope_tmp[:, 2 * b + 1], bank, rope_a[:, 0, cols], ALU.mult).then_inc(rope_b_s, 1)
                        dve.wait_ge(rope_a_s, n + 1)
                        nc.vector.tensor_tensor(rope_tmp[:, 2 * b], rope_tmp[:, 2 * b], rope_a[:, 1, cols], ALU.mult).then_inc(rope_c_s, 1)
                        dve.wait_ge(rope_b_s, n + 1)
                        dve.wait_ge(rope_c_s, n + 1)
                        dst = q_t[:, j, cols] if j < 2 else k_t[:, j - 2, DH + h * HALF:DH + (h + 1) * HALF]
                        nc.vector.tensor_tensor(dst, rope_tmp[:, 2 * b], rope_tmp[:, 2 * b + 1], ALU.add).then_inc(dve_free, 1)

            def group_attention(layer, g):
                u0 = unit0[(layer, g)]
                nch = window(g, (0, 0))[2]
                w = nch * P

                def step(v, ahead, now, behind):
                    if ahead:
                        x = plus(v, 1)
                        b = x[1] % 2
                        u = u0 + idx(x)
                        dve.wait_ge(scores, u + 1)
                        if u0 > 0 or not early(x, 2):
                            dve.wait_ge(probs_t, u - 1)
                        if layer == 0 and not early((x[0], x[1] + u0), 2):
                            dve.wait_ge(stat_kept, u - 1 if g != "mem" else NG * TT)
                        if g != "mem":
                            dve.wait_ge(mask_in[b], 16 * (x[0] + x[1] // 2) + 16 * (g * TT // 2 + 1))
                        fence(dve)
                        for h in range(GH):
                            last = nc.vector.tensor_tensor_reduce(
                                out=prob[:, b, h * 256:h * 256 + w], in0=ps[:, 2 * b + h // 2, (h % 2) * 256:(h % 2) * 256 + w],
                                in1=masked_by[:, b, 0:w], scale=1.0, scalar=LOWEST, op0=ALU.add, op1=ALU.max,
                                accum_out=stat[:, b, 0, h:h + 1])
                        last.then_inc(masked, 1)
                        dve.wait_ge(masked, staged0[(layer, g)] + idx(x) + 1)
                        nc.vector.tensor_scalar(neg_max[:, b], stat[:, b, 0], -SCALE_A, None, ALU.mult).then_inc(max_ready, 1)
                    if now:
                        u = u0 + idx(v)
                        b = v[1] % 2
                        dve.wait_ge(probs_t, u + 1)
                        if g == "mem":
                            dve.wait_ge(o_out, u - 1)
                            nc.vector.reciprocal(recip_den[:, b], stat[:, b, 1]).then_inc(den_ready, 1)
                        if u0 > 0 or not early(v, 2):
                            dve.wait_ge(pv, u - 1)
                        if nch == 2:
                            nc.vector.tensor_copy(prob_t[:, b, HALF:], ps[:, 5]).then_inc(pt_dve, 1)
                        else:
                            nc.vector.tensor_copy(prob_t[:, b, HALF:].rearrange("p (a b) -> p a b", a=2)[:, :, 0:P],
                                                  ps[:, 5].rearrange("p (a b) -> p a b", a=2)[:, :, 0:P]).then_inc(pt_dve, 1)
                    if behind and g == "mem":
                        x = plus(v, -1)
                        b = x[1] % 2
                        dve.wait_ge(pv, u0 + idx(x) + 1)
                        dve.wait_ge(den_ready, DEN0[layer] + idx(x) + 1)
                        off = GW if layer == 0 else MLA_H * DH
                        nc.vector.tensor_tensor(
                            mix[layer][:, bass.ds(idx(x), 1), off:off + GW].rearrange("p a (h c) -> p (a h) c", h=GH),
                            ps[:, 6 + b, 0:GW].rearrange("p (h c) -> p h c", h=GH),
                            recip_den[:, b].rearrange("p (h a) -> p h a", a=1).to_broadcast([P, GH, DH]), ALU.mult).then_inc(o_out, 1)
                pipeline(dve, step)

            def zero_masks(l):
                dve.wait_ge(masked, staged0[(l, "mem")])
                nc.vector.memset(masked_by, 0.0).then_inc(mask_zero, 1)
                dve.wait_ge(mask_zero, l + 1)

            def merge():
                dve.wait_ge(merge_in, 48)
                dve.wait_ge(o_out, LAYER_UNITS[0])
                mx = merged[:, :, :, GW:GW + GH]
                dn = merged[:, :, :, GW + GH:]
                merge_link(nc.vector.tensor_tensor(merge_m[:], mx[:, :, 0], mx[:, :, 1], ALU.max))
                merge_link(nc.vector.tensor_tensor(merge_m[:], merge_m[:], mx[:, :, 2], ALU.max))
                for g in range(NG):
                    last = nc.vector.tensor_tensor(merge_e[:, :, g], mx[:, :, g], merge_m[:], ALU.subtract)
                last.then_inc(merge_diff, 1)
                dve.wait_ge(merge_exp, 1)
                merge_link(nc.vector.tensor_tensor(dn, dn, merge_e[:], ALU.mult))
                merge_link(nc.vector.tensor_tensor(merge_m[:], dn[:, :, 0], dn[:, :, 1], ALU.add))
                merge_link(nc.vector.tensor_tensor(merge_m[:], merge_m[:], dn[:, :, 2], ALU.add))
                merge_link(nc.vector.reciprocal(merge_m[:], merge_m[:]))
                for g in range(NG):
                    last = nc.vector.tensor_tensor(merge_e[:, :, g], merge_e[:, :, g], merge_m[:], ALU.mult)
                merge_link(last)
                for t in range(TT):
                    for g in range(NG):
                        o = merged[:, t, g, 0:GW].rearrange("p (h c) -> p h c", h=GH)
                        wt = merge_e[:, t, g].rearrange("p (h a) -> p h a", a=1).to_broadcast([P, GH, DH])
                        last = nc.vector.tensor_tensor(o, o, wt, ALU.mult)
                merge_link(last)
                m2 = mix[0][:, :, 0:GW]
                merge_link(nc.vector.tensor_tensor(m2, merged[:, :, 0, 0:GW], merged[:, :, 1, 0:GW], ALU.add))
                nc.vector.tensor_tensor(m2, m2, merged[:, :, 2, 0:GW], ALU.add).then_inc(mix_done, 1)

            def tile_stats(i, t):
                n = i * TT + t
                dve.wait_ge(z_done, n + 1)
                for h in range(2):
                    last = nc.vector.bn_stats(stats[:, t % 2, h], X[:, t, h * HALF:(h + 1) * HALF])
                last.then_inc(st_done, 1)
                dve.wait_ge(st_done, n + 1)
                nc.vector.bn_aggr(mean_var[:, t], stats[:, t % 2]).then_inc(mv_done, 1)

            def tile_rstd(i, t):
                dve.wait_ge(sd_done, i * TT + t + 1)
                ln_link(nc.vector.reciprocal(rstd[:, t, 0:1], std[:, t:t + 1]))
                nc.vector.scalar_tensor_tensor(out=rstd[:, t, 1:2], in0=mean_var[:, t, 0:1], scalar=-1.0, in1=rstd[:, t, 0:1],
                                               op0=ALU.mult, op1=ALU.mult).then_inc(rs_done, 1)

            def token_copies(i, t):
                n = i * TT + t + 1
                dve.wait_ge(xt_ps, n)
                nc.vector.tensor_copy(XT[:, 4:8, t * P:(t + 1) * P], ps[:, 7].rearrange("p (a b) -> p a b", a=4)).then_inc(xt_dve, 1)

            def out_projection(l):
                i = 2 * l
                if l == 0:
                    dve.wait_ge(x_res_in, 16)
                dve.wait_ge(router_in, 64 * (l + 1))
                for t in range(TT + 2):
                    if t < TT:
                        dve.wait_ge(y_ps, l * TT + t + 1)
                        nc.vector.scalar_tensor_tensor(out=X[:, t], in0=X[:, t], scalar=ALPHA,
                                                       in1=ps[:, 2 * (t % 2):2 * (t % 2) + 2].rearrange("p a b -> p (a b)"),
                                                       op0=ALU.mult, op1=ALU.add).then_inc(z_done, 1)
                        tile_stats(i, t)
                    if 1 <= t < TT + 1:
                        tile_rstd(i, t - 1)
                    if t >= 2:
                        token_copies(i, t - 2)
                        dve.wait_ge(r_ps, l * TT + t - 1)
                        nc.vector.tensor_tensor(logits[:, t - 2], ps[:, 5, 256:256 + NR], b_router[:], ALU.add).then_inc(r_out, 1)

            def routing(l):
                link = route_link
                V = nc.vector
                TTN = [P, TT, NE]
                g_l = logits[:, :, 0:N_GRP]
                e_l = logits[:, :, N_GRP:]
                dve.wait_ge(r_out, TT * (l + 1))

                def bc(x, n):
                    return x.rearrange("p (t a) -> p t a", a=1).to_broadcast([P, TT, n])

                def first_max(src, n, tie, m, hot, scratch):
                    link(V.tensor_reduce(m, src, AX.X, ALU.max))
                    link(V.tensor_tensor(hot, src, bc(m, n), ALU.is_equal))
                    link(V.tensor_tensor(hot, hot, tie.rearrange("p (a n) -> p a n", a=1).to_broadcast([P, TT, n]), ALU.mult))
                    link(V.tensor_reduce(scratch, hot, AX.X, ALU.max))
                    link(V.tensor_tensor(hot, hot, bc(scratch, n), ALU.is_equal))

                dve.wait_ge(table_in, 16 * (l + 1))
                gm, sc, gs, m1, m2, e21, w1 = (r_one[:, n] for n in range(7))
                r_nov, r_ovs = r_exp[:, 0], r_exp[:, 1]
                first_max(g_l, N_GRP, T_TIEG, gm, hot_g, sc)
                V.tensor_tensor(r_eg[:], g_l, bc(gm, N_GRP), ALU.subtract).then_inc(route_exp_in, 1)
                link(V.tensor_copy(rt[0][:, :, :].rearrange("p t (g e) -> p t g e", g=N_GRP),
                                   hot_g.rearrange("p t (g a) -> p t g a", a=1).to_broadcast([P, TT, N_GRP, EPG])))
                link(V.tensor_tensor(rt[1], e_l, rt[0], ALU.mult))
                link(V.tensor_scalar(rt[0], rt[0], BIG, -BIG, ALU.mult, ALU.add))
                link(V.tensor_tensor(rt[1], rt[1], rt[0], ALU.add))
                first_max(rt[1], NE, T_TIEE, m1, rt[2], sc)
                link(V.tensor_scalar(rt[3], rt[2], -2 * BIG, None, ALU.mult))
                link(V.tensor_tensor(rt[1], rt[1], rt[3], ALU.add))
                first_max(rt[1], NE, T_TIEE, m2, rt[3], sc)
                V.tensor_tensor(e21, m2, m1, ALU.subtract).then_inc(route_exp_in, 1)
                V.tensor_tensor(hot_both, rt[2], rt[3], ALU.add).then_inc(route_hot, 1)
                dve.wait_ge(route_exp, 2 * l + 2)
                link(V.tensor_reduce(gs, r_eg[:], AX.X, ALU.add))
                link(V.tensor_scalar(w1, e21, 1.0, None, ALU.add))
                link(V.tensor_tensor(gs, gs, w1, ALU.mult))
                link(V.reciprocal(gs, gs))
                link(V.tensor_copy(gates[:, :, 0], gs))
                link(V.tensor_tensor(gates[:, :, 1], gs, e21, ALU.mult))
                dve.wait_ge(rank_ps, l + 1)
                link(V.tensor_copy(rank, ps[:, 0, 0:TT * NE].rearrange("p (t e) -> p t e", e=NE)))
                link(V.tensor_copy(counts, ps[:, 1, 0:NE]))
                c3 = big_tmp.rearrange("p a b -> p (a b)")[:, 0:NE * NCHUNK].rearrange("p (a b) -> p a b", b=NCHUNK)
                link(V.tensor_tensor(c3, counts.rearrange("p (e a) -> p e a", a=1).to_broadcast([P, NE, NCHUNK]),
                                     T_THR.rearrange("p (a n) -> p a n", a=1).to_broadcast([P, NE, NCHUNK]), ALU.is_gt))
                link(V.tensor_reduce(r_nov, c3, AX.X, ALU.add))
                link(V.tensor_tensor(big_tmp, r_nov.rearrange("p (a e) -> p a e", a=1).to_broadcast([P, NE, NE]), T_TRI, ALU.mult))
                link(V.tensor_reduce(r_ovs, big_tmp, AX.X, ALU.add))
                link(V.tensor_tensor(r_nov, r_ovs, r_nov, ALU.add))
                c4 = big_tmp.rearrange("p a b -> p (a b)")[:, 0:NE * NOVER].rearrange("p (a b) -> p a b", b=NE)
                link(V.tensor_tensor(c4, r_nov.rearrange("p (a e) -> p a e", a=1).to_broadcast([P, NOVER, NE]),
                                     T_CHUNK.rearrange("p (n a) -> p n a", a=1).to_broadcast([P, NOVER, NE]), ALU.is_le))
                link(V.tensor_reduce(r_chunk[:, 0:NOVER], c4, AX.X, ALU.add))
                link(V.tensor_scalar(r_chunk[:, 0:NOVER], r_chunk[:, 0:NOVER], float(NE - 1), None, ALU.min))
                link(V.tensor_copy(r_chunk[:, NOVER:NOVER + 1], r_nov[:, NE - 1:NE]))
                link(V.tensor_copy(over_i[:], r_chunk[:]))
                link(V.tensor_tensor(r_ovs, r_ovs, T_BASE, ALU.subtract))
                link(V.tensor_scalar(r_ovs, r_ovs, float(CAP), float((NE - 1) * CAP), ALU.mult, ALU.add))
                link(V.tensor_scalar(rt[4], rank, float(CAP), None, ALU.is_ge))
                link(V.tensor_tensor(rt[4], rt[4], r_ovs.rearrange("p (a e) -> p a e", a=1).to_broadcast(TTN), ALU.mult))
                link(V.tensor_tensor(rank, rank, rt[4], ALU.add))
                link(V.tensor_scalar(rt[4], T_BASE.rearrange("p (a e) -> p a e", a=1).to_broadcast(TTN), float(CAP), None, ALU.mult))
                link(V.tensor_tensor(rank, rank, rt[4], ALU.add))
                for k in range(2):
                    link(V.tensor_tensor(rt[5], rank, rt[2 + k], ALU.mult))
                    link(V.tensor_reduce(r_slot[:, k], rt[5], AX.X, ALU.add))
                V.tensor_copy(slots_i[:].rearrange("p t k -> p k t"), r_slot[:]).then_inc(route_done, 1)

            def experts(l):
                n0 = NE * l
                r0 = RING_USES * l

                def rows(e, b):
                    dve.wait_ge(xst_ps, n0 + e + 1)
                    nc.vector.tensor_copy(xs_t[b].rearrange("p (a c) n -> p a (c n)", a=2), ps[:, 0:2, 0:4 * CAP]).then_inc(xst_out, 1)

                def hidden(e, b):
                    dve.wait_ge(silu_done, n0 + e + 1)
                    dve.wait_ge(up_ps, n0 + e + 1)
                    nc.vector.tensor_tensor(h_t[b], sil[b], ps[:, 3, 0:4 * CAP].rearrange("p (a b) -> p a b", a=4), ALU.mult).then_inc(h_done, 1)

                def expert(e, b, n, more):
                    hidden(e, b)
                    if more:
                        rows(e + 1, 1 - b)
                    dve.wait_ge(down_ps, n0 + e + 1)
                    if not (isinstance(n, int) and n == 0):
                        dve.wait_ge(ys_out[b], 16 * n)
                    nc.vector.tensor_copy(ys[0:CAP, b, HALF:], ps[0:CAP, 5 + 2 * b]).then_inc(y_dve, 1)

                rows(0, 0)
                expert(0, 0, r0, True)
                expert(1, 1, r0, True)
                with dve.Fori(0, NE // 2 - 2) as i:
                    expert(2 * i + 2, 0, r0 + i + 1, True)
                    expert(2 * i + 3, 1, r0 + i + 1, True)
                expert(NE - 2, 0, r0 + NE // 2 - 1, True)
                expert(NE - 1, 1, r0 + NE // 2 - 1, False)
                o = ov[l]
                for b in range(2):
                    dve.wait_ge(ys_out[b], 16 * 16 * (l + 1))
                n_over = dve.value_load(over_i[0:1, NOVER:NOVER + 1], min_val=0, max_val=NOVER)
                with dve.If(n_over > 0):
                    with dve.Fori(0, n_over) as j:
                        dve.wait_ge(o["xst"], j + 1)
                        nc.vector.tensor_copy(xs_t[0].rearrange("p (a c) n -> p a (c n)", a=2), ps[:, 0:2, 0:4 * CAP]).then_inc(o["xsto"], 1)
                        dve.wait_ge(o["silu"], j + 1)
                        dve.wait_ge(o["up"], j + 1)
                        nc.vector.tensor_tensor(h_t[0], sil[0], ps[:, 3, 0:4 * CAP].rearrange("p (a b) -> p a b", a=4), ALU.mult).then_inc(o["h"], 1)
                        dve.wait_ge(o["down"], j + 1)
                        nc.vector.tensor_copy(ys[0:CAP, 0], ps[0:CAP, 4:6].rearrange("p a b -> p (a b)")).then_inc(o["y"], 1)
                with dve.Else():
                    dve.nop()
                dve.nop()

            def combine(l):
                i = 2 * l + 1
                for t in range(TT + 2):
                    if t < TT:
                        n = TT * l + t
                        b = t % 2
                        dve.wait_ge(yin[b], 32 * (4 * l + t // 2 + 1))
                        nc.vector.tensor_scalar(X[:, t], X[:, t], ALPHA, None, ALU.mult).then_inc(fz, 1)
                        dve.wait_ge(fz, 2 * n + 1)
                        nc.vector.scalar_tensor_tensor(out=X[:, t], in0=y_in[:, b, 0], scalar=gates[:, t, 0:1], in1=X[:, t],
                                                       op0=ALU.mult, op1=ALU.add).then_inc(fz, 1)
                        dve.wait_ge(fz, 2 * n + 2)
                        nc.vector.scalar_tensor_tensor(out=X[:, t], in0=y_in[:, b, 1], scalar=gates[:, t, 1:2], in1=X[:, t],
                                                       op0=ALU.mult, op1=ALU.add).then_inc(z_done, 1)
                        tile_stats(i, t)
                    if 1 <= t < TT + 1:
                        tile_rstd(i, t - 1)
                    if l == 0 and t >= 2:
                        token_copies(i, t - 2)

            def latent_norms():
                V = nc.vector
                dve.wait_ge(rms_std, 1)
                V.reciprocal(rms_ss[:], rms_ss[:]).then_inc(rms_r, 1)
                dve.wait_ge(rms_r, 1)
                for t in range(TT):
                    V.tensor_scalar(latent[:, t, 0:QL], latent[:, t, 0:QL], rms_ss[:, t, 0:1], None, ALU.mult)
                    V.tensor_scalar(latent[:, t, QL:QL + KVL], latent[:, t, QL:QL + KVL], rms_ss[:, t, 1:2], None, ALU.mult).then_inc(lat_scaled, 1)
                mem_values(1)
                dve.wait_ge(lat_t, TT)
                rows = slice(DH, QKB)
                step = chain(k_rot_step, [0])
                for h in range(2):
                    cols = slice(h * HALF, (h + 1) * HALF)
                    step(V.stream_shuffle(rope_tmp_b[rows, 0], k_rot[rows, cols], swap_b))
                    step(V.tensor_tensor(rope_tmp_b[rows, 0], rope_tmp_b[rows, 0], rope_b[rows, 1, cols], ALU.mult))
                    step(V.tensor_tensor(rope_tmp_b[rows, 1], k_rot[rows, cols], rope_b[rows, 0, cols], ALU.mult))
                    for hb in range(2):
                        last = V.tensor_tensor(k_head[rows, hb, cols], rope_tmp_b[rows, 0], rope_tmp_b[rows, 1], ALU.add)
                    step(last)
                V.tensor_copy(recip_den[:, 0, 0:1], rms_ss[:, 0, 0:1]).then_inc(k_rot_done, 1)

            def head_rope(h, hb, j):
                V = nc.vector
                rows, cols = slice(DH, QKB), slice(j * HALF, (j + 1) * HALF)
                n = 2 * h + j + 1
                dve.wait_ge(head_ps, 4 * h + j + 1)
                dve.wait_ge(scores, unit0[(1, "mla")] - TT + TT * h)
                fence(dve)
                V.stream_shuffle(rope_tmp_b[rows, 0], ps[rows, 7], swap_b).then_inc(hr_a, 1)
                V.tensor_tensor(rope_tmp_b[rows, 1], ps[rows, 7], rope_b[rows, 0, cols], ALU.mult).then_inc(hr_b, 1)
                dve.wait_ge(hr_a, n)
                V.tensor_tensor(rope_tmp_b[rows, 0], rope_tmp_b[rows, 0], rope_b[rows, 1, cols], ALU.mult).then_inc(hr_c, 1)
                dve.wait_ge(hr_b, n)
                dve.wait_ge(hr_c, n)
                V.tensor_tensor(q_head[rows, hb, cols], rope_tmp_b[rows, 0], rope_tmp_b[rows, 1], ALU.add).then_inc(head_dve, 1)

            def latent_attention():
                u0 = unit0[(1, "mla")]
                for j in range(2):
                    head_rope(0, 0, j)

                def step(v, ahead, now, behind):
                    if ahead:
                        w = plus(v, 1)
                        n, b = latent_idx(w), w[1] % 2
                        dve.wait_ge(scores, u0 + n + 1)
                        nc.vector.tensor_reduce(stat[:, b, 0, 0:1], ps[:, 2 * b:2 * b + 2].rearrange("p a b -> p (a b)"), AX.X, ALU.max).then_inc(row_max, 1)
                        dve.wait_ge(row_max, n + 1)
                        nc.vector.tensor_scalar(neg_max[:, b, 0:1], stat[:, b, 0, 0:1], -SCALE_B, None, ALU.mult).then_inc(max_ready, 1)
                    if now:
                        n, b = latent_idx(v), v[1] % 2
                        dve.wait_ge(probs_t, u0 + n + 1)
                        dve.wait_ge(o_out, u0 + n - 1)
                        nc.vector.reciprocal(recip_den[:, b, 0:1], stat[:, b, 1, 0:1]).then_inc(den_ready, 1)
                        dve.wait_ge(pv, u0 + n - 1)
                        nc.vector.tensor_copy(prob_t[:, b, HALF:], ps[:, 5]).then_inc(pt_dve, 1)
                        if projects(v) and v[1] % TT < 4:
                            head_rope(2 * v[0] + v[1] // TT + 1, (v[1] // TT + 1) % 2, v[1] % TT - 2)
                    if behind:
                        w = plus(v, -1)
                        n, b, t = latent_idx(w), w[1] % 2, w[1] % TT
                        h = 2 * w[0] + w[1] // TT
                        dve.wait_ge(pv, u0 + n + 1)
                        dve.wait_ge(den_ready, DEN0["mla"] + n + 1)
                        nc.vector.tensor_scalar(mix[1][:, t, bass.ds(h * DH, DH)], ps[:, 6, b * DH:(b + 1) * DH], recip_den[:, b, 0:1], None, ALU.mult).then_inc(o_out, 1)
                latent_pipeline(dve, step)

            dve.wait_ge(zeroed, 5)
            mem_values(0)
            for g in range(NG):
                group_rope(g)
                group_attention(0, g)
            zero_masks(0)
            group_attention(0, "mem")
            merge()
            out_projection(0)
            routing(0)
            experts(0)
            combine(0)
            latent_norms()
            latent_attention()
            zero_masks(1)
            group_attention(1, "mem")
            out_projection(1)
            routing(1)
            experts(1)
            combine(1)


def rope_table(dim, rows, reps, positions):
    inv = np.float32(ROPE_THETA) ** (-np.arange(0, dim, 2, dtype=np.float32) / np.float32(dim))
    ang = positions.astype(np.float32)[None, :] * inv.astype(np.float32)[:, None]
    c, s = np.cos(ang), np.sin(ang)
    cos = np.ones((rows, positions.size), np.float32)
    sin = np.zeros((rows, positions.size), np.float32)
    cos[:dim // 2], cos[dim // 2:dim] = c, c
    sin[:dim // 2], sin[dim // 2:dim] = -s, s
    return np.stack([np.tile(cos, (reps, 1)), np.tile(sin, (reps, 1))])


def group_order(g):
    dil = DIL_GROUPS[g][1]
    return np.arange(S).reshape(S // dil, dil).T.reshape(-1)


def group_masks():
    m = np.full((NG, TT, P, 256), -BIG, np.float32)
    q = np.arange(P)[:, None]
    for g, (window, dil) in enumerate(DIL_GROUPS):
        radius, length = window // (2 * dil), S // dil
        for u in range(TT):
            if g == 0:
                qpos, kpos, width = u * P + q, u * P - DH + np.arange(256)[None, :], 256
                ok = (np.abs(qpos - kpos) <= radius) & (kpos >= 0) & (kpos < length)
            elif g == 1:
                qpos, kpos, width = (u % 2) * P + q, np.arange(256)[None, :], 256
                ok = np.abs(qpos - kpos) <= radius
            else:
                kpos, width = np.arange(P)[None, :], P
                ok = (q // length == kpos // length) & (np.abs(q - kpos) <= radius)
            m[g, u, :, :width][ok] = 0.0
    return m


def constants():
    tok = (np.arange(TT)[None, :, None] * P + np.arange(P)[:, None, None])
    infos = np.zeros((P, TT, 2, 2), np.int32)
    infos[..., 0] = tok
    infos[..., 1] = tok + S * np.arange(2)[None, None, :]
    table = np.concatenate([
        np.arange(N_GRP, 0, -1), np.arange(NE, 0, -1), np.arange(NE),
        (np.arange(NE)[None, :] < np.arange(NE)[:, None]).astype(int).reshape(-1),
        CAP * np.arange(1, NCHUNK + 1), np.arange(NOVER),
    ]).astype(np.float32)[None, :]
    return {
        "ident": np.eye(P, dtype=np.float32),
        "tri": (np.arange(P)[:, None] < np.arange(P)[None, :]).astype(np.float32),
        "nowhere": np.full((SLOTS, 2), NOWHERE, np.int32),
        "infos": infos,
        "route_table": table,
        "rope_a": np.stack([rope_table(DH // 4, DH, 2, group_order(g)) for g in range(NG)]),
        "rope_b": rope_table(ROPE_B, ROPE_B, 1, np.arange(S)),
        "masks": group_masks(),
    }


WEIGHTS = ("a_w_in", "a_w_out", "b_w_in", "b_w_qb", "b_w_kvb", "b_w_out", "mem_w_kv", "ln_mix_g", "ln_mix_b",
           "ln_ffn_g", "ln_ffn_b", "router_w_grp", "router_b_grp", "router_w_exp", "router_b_exp",
           "exp_w_gate", "exp_w_up", "exp_w_down")


def kernel(**inputs):
    import concourse.bacc as bacc
    from concourse.bass_utils import run_bass_kernel_spmd

    a = {n: np.ascontiguousarray(inputs[n]) for n in WEIGHTS}
    x = np.ascontiguousarray(inputs["x"])[0]
    a["x"] = x
    a["x_t"] = np.stack([np.pad(x[group_order(g)].T, ((0, 0), (DH, DH))) for g in range(NG)])
    a["mem_t"] = np.ascontiguousarray(np.asarray(inputs["mem"])[0].T)
    a["b_norms"] = np.ascontiguousarray(np.concatenate([
        np.asarray(inputs["b_q_norm"])[0].reshape(2, P), np.asarray(inputs["b_kv_norm"])[0].reshape(1, P)]).T)
    a.update(constants())
    nc = bacc.Bacc("TRN2", target_bir_lowering=False, num_devices=1)
    io, arrays = {}, {}
    for n, v in a.items():
        arrays[f"in_{n}"] = v
        io[n] = nc.dram_tensor(f"in_{n}", v.shape, mybir.dt.from_np(v.dtype), kind="ExternalInput").ap()
    io["out"] = nc.dram_tensor("out_x", (S, D), F32, kind="ExternalOutput").ap()
    build(nc, io)
    r = run_bass_kernel_spmd(nc, [arrays], core_ids=[0])
    return r.results[0]["out_x"].reshape(1, S, D)
```

```python
import numpy as np
from contextlib import ExitStack

import concourse.bass as bass
from concourse import mybir

F32 = mybir.dt.float32
I32 = mybir.dt.int32
ALU = mybir.AluOpType
ACT = mybir.ActivationFunctionType
AX = mybir.AxisListType

P = 128
D = 1024
S = 1024
DEPTH = 2
KT = D // P
TT = S // P
HALF = 512
DH = 64
DIL_GROUPS = ((128, 1), (512, 4), (2048, 16))
NG = len(DIL_GROUPS)
GH = 4
GW = GH * DH
PADW = S + 2 * DH
MEM = 256
MLA_H = 8
QL, KVL, ROPE_B = 256, 128, 32
LAT = QL + KVL + ROPE_B
QKB = DH + ROPE_B
N_GRP, EPG = 4, 8
NE = N_GRP * EPG
NR = N_GRP + NE
DE = 512
ALPHA = (2 * DEPTH) ** 0.25
LN_EPS, RMS_EPS = 1e-5, 1e-6
SCALE_A = DH ** -0.5
SCALE_B = QKB ** -0.5
ROPE_THETA = 500000.0
BIG = 1e30
LOWEST = -3e38

CAP = 104
NOVER = (2 * S) // (CAP + 1)
NCHUNK = S // CAP
SLOTS = NOVER * CAP
NOWHERE = 1 << 20
OSTR = GW + 2 * GH
PART = 4096


def build(nc, io):
    with ExitStack() as ctx:
        def sb(name, shape, dt=F32):
            return ctx.enter_context(nc.sbuf_tensor(name, shape, dt))

        def sem(name):
            return ctx.enter_context(nc.semaphore(name))

        ring = sb("ring", [P, 6 * PART])
        arena = sb("arena", [P, 88 * 256])
        o_stage = sb("o_stage", [P, 2, OSTR])
        km_t = sb("mem_keys_t", [P, 2, MEM])
        v_mem = sb("mem_values", [P, 2, GW])
        q_stage = sb("q_stage", [P, 2, GH, P])
        ln_gb = sb("ln_gb", [P, 2, D])
        ident = sb("ident", [P, P])
        tri = sb("tri", [P, P])
        ones = sb("ones", [P, P])
        w_router = sb("w_router", [P, KT, NR])
        b_router = sb("b_router", [P, NR])
        stat = sb("max_and_sum", [P, 2, 2, GH])
        neg_max = sb("neg_max", [P, 2, GH])
        recip_den = sb("recip_den", [P, 2, GH])
        stats = sb("ln_stats", [P, 2, 2, 6])
        mean_var = sb("ln_mean_var", [P, TT, 2])
        std = sb("ln_std", [P, TT])
        rstd = sb("ln_rstd", [P, TT, 2])
        eps = sb("eps", [P, 2])
        gates = sb("gates", [P, TT, 2])
        slots_i = sb("slots_i", [P, TT, 2], I32)
        infos = sb("infos", [P, TT, 2, 2], I32)
        g_idx = sb("gather_idx", [P, 2], I32)
        s_idx = sb("scatter_idx", [P, 2], I32)
        over_idx = sb("over_idx", [P, 2], I32)
        over_i = sb("over_table", [P, NOVER + 1], I32)
        rms_ss = sb("rms_ss", [P, TT, 2])
        rms_g = sb("rms_g", [P, 3])
        merge_e = sb("merge_e", [P, TT, NG, GH])
        merge_m = sb("merge_m", [P, TT, GH])
        logits = sb("logits", [P, TT, NR])

        ps = ctx.enter_context(nc.psum_tensor("banks", [P, 8, HALF], F32))

        def at(kb, *shape, base=arena):
            n = int(np.prod(shape))
            off = int(kb * 256)
            v = base[:, off:off + n]
            if len(shape) == 1:
                return v
            names = "abcd"[:len(shape)]
            return v.rearrange(f"p ({' '.join(names)}) -> p {' '.join(names)}",
                               **{c: s for c, s in zip(names, shape)})

        def ring_at(kb, *shape):
            return at(kb, *shape, base=ring)

        X = at(0, TT, D)
        XT = at(32, KT, S)
        q_t = at(32, 2, S)
        k_t = at(40, 2, PADW)
        v_a = at(49, 9, GW)
        merged = at(32, TT, NG, OSTR)
        qm_t = at(64, 2, S)
        masked_by = at(60, 2, 256)
        prob = at(72, 2, S)
        prob_t = at(80, 2, S)
        rope_a = at(72, 2, S)
        rope_tmp = at(80, 4, HALF)
        x_t = [ring_at(0, KT, PADW), ring_at(36, KT, PADW)]
        w_a = [ring_at(72, 3, KT, GW), at(0, 3, KT, GW)]
        w_qm_a = at(24, KT, GW)
        mem_w = [at(0, KT, 2 * GW), ring_at(48, KT, 2 * GW)]
        mem_t = [at(16, KT, MEM), ring_at(64, KT, MEM)]
        w_out = [ring_at(80, 4, D), ring_at(64, 6, D)]
        mix = [ring_at(0, TT, 512), ring_at(0, TT, 768)]
        w_in_b = ring_at(72, KT, LAT + GW)
        rope_b = ring_at(24, 2, S)
        q_head = ring_at(32, 2, S)
        k_head = ring_at(40, 2, S)
        w_q_head = ring_at(48, 2, 2, QKB)
        w_k_head = ring_at(49.5, 2, DH)
        w_v = ring_at(50, MLA_H, DH)
        rope_tmp_b = ring_at(52, 2, HALF)
        latent = ring_at(0, TT, LAT)
        v_b = at(32, TT, MLA_H * DH)
        cq_t = at(48, 2, S)
        ckv_t = at(56, S)
        k_rot = at(60, S)
        square = ring_at(14, 2, QL + KVL)
        mix_t = at(72, 2, 6, P)
        xs = at(32, 2, D)
        xs_t = [at(40, KT, CAP), at(44, KT, CAP)]
        h_t = [at(48, 4, CAP), at(50, 4, CAP)]
        sil = [at(52, 4, CAP), at(54, 4, CAP)]
        ys = at(56, 2, D)
        y_in = at(64, 2, 2, D)

        og = nc.dram_tensor("group_results", [NG, S, OSTR], F32).ap()
        x1_d = [nc.dram_tensor(f"moe_in_{l}", [S, D], F32).ap() for l in range(DEPTH)]
        slot_d = [nc.dram_tensor(f"overflow_rows_{l}", [SLOTS, 2], I32).ap() for l in range(DEPTH)]
        y_d = [nc.dram_tensor(f"expert_out_{l}", [2 * S, D], F32).ap() for l in range(DEPTH)]

        consts_in = sem("consts_in")
        infos_in = sem("infos_in")
        zeroed = sem("zeroed")
        fenced = {e: sem(f"fenced_{n}") for e, n in ((nc.sync.engine, "sp"), (nc.gpsimd.engine, "pool"), (nc.vector.engine, "dve"))}
        slots_cleared = sem("slots_cleared")
        mem_in = sem("mem_in")
        mem_v_in = sem("mem_value_weights_in")
        mem_proj = sem("mem_proj")
        mem_kv_act = sem("mem_kv_act")
        mem_kv_dve = sem("mem_kv_dve")
        x_in = [sem("x_in0"), sem("x_in1")]
        x_rest_in = [sem("x_rest_in0"), sem("x_rest_in1")]
        w_in = [sem("w_in0"), sem("w_in1")]
        wv_in = [sem("wv_in0"), sem("wv_in1")]
        rope_in = sem("rope_in")
        wqm_in = sem("wqm_in")
        act_full = sem("proj_for_act")
        act_free = sem("proj_freed_by_act")
        dve_full = sem("proj_for_dve")
        dve_free = sem("proj_freed_by_dve")
        rope_a_s = sem("rope_shuffled")
        rope_b_s = sem("rope_cos")
        rope_c_s = sem("rope_sin")
        q_staged = sem("q_staged")
        mask_in = [sem("mask_in0"), sem("mask_in1")]
        scores = sem("scores")
        masked = sem("masked")
        max_ready = sem("max_ready")
        stat_kept = sem("stat_kept")
        probs = sem("probs")
        probs_t = sem("probs_transposed")
        pt_act = sem("pt_copied_act")
        pt_dve = sem("pt_copied_dve")
        pv = sem("pv")
        o_out = sem("o_out")
        o_stored = [sem("o_stored0"), sem("o_stored1")]
        mask_zero = sem("mask_zero")
        den_ready = sem("den_ready")
        merge_in = sem("merge_in")
        mstep = sem("merge_step")
        merge_diff = sem("merge_diff")
        merge_exp = sem("merge_exp")
        mix_done = sem("mix_done")
        x_res_in = sem("x_res_in")
        wout_in = sem("wout_in")
        gb_in = sem("gb_in")
        router_in = sem("router_in")
        mixt_ps = sem("mixt_ps")
        mixt_act = sem("mixt_act")
        y_ps = sem("y_ps")
        z_done = sem("z_done")
        st_done = sem("stats_done")
        mv_done = sem("mean_var_done")
        sd_done = sem("std_done")
        rs_step = sem("rstd_step")
        rs_done = sem("rstd_done")
        norm_done = sem("norm_done")
        gmul_done = sem("gmul_done")
        x_ready = sem("x_ready")
        x_last = sem("x_last_ready")
        last_gmul = sem("last_gmul_done")
        xt_ps = sem("xt_ps")
        xt_act = sem("xt_act")
        xt_dve = sem("xt_dve")
        r_ps = sem("router_ps")
        r_out = sem("router_out")
        x1_stored = sem("x1_stored")
        rstep = sem("routing_step")
        route_exp_in = sem("route_exp_in")
        route_exp = sem("route_exp")
        route_hot = sem("route_hot")
        rank_ps = sem("rank_ps")
        route_done = sem("route_done")
        table_in = sem("table_in")
        index_hot = sem("index_one_hots")
        index_ps = sem("index_ps")
        over_done = sem("overflow_planned")
        x_scaled = sem("x_scaled")
        ring_in = [sem(f"ring_in{i}") for i in range(6)]
        idx_set = sem("idx_set")
        xs_in = [sem("xs_in0"), sem("xs_in1")]
        xst_ps = sem("xst_ps")
        xst_out = sem("xst_out")
        gate_ps = sem("gate_ps")
        up_ps = sem("up_ps")
        silu_done = sem("silu_done")
        h_done = sem("h_done")
        down_ps = sem("down_ps")
        y_act = sem("y_act")
        y_dve = sem("y_dve")
        ys_out = [sem("ys_out0"), sem("ys_out1")]
        yin = [sem("y_in0"), sem("y_in1")]
        fz = sem("final_z_step")
        w_b_in = sem("w_in_b_in")
        b_in = sem("layer_b_in")
        hw_in = [sem("head_weights_in0"), sem("head_weights_in1")]
        head_ps = sem("head_ps")
        row_max = sem("row_max")
        hr_a = sem("head_rope_shuffled")
        hr_b = sem("head_rope_cos")
        hr_c = sem("head_rope_sin")
        k_rot_step = sem("k_rot_step")
        k_rot_done = sem("k_rot_done")
        rms_std = sem("rms_std")
        rms_r = sem("rms_r")
        lat_scaled = sem("lat_scaled")
        lat_ps = sem("lat_ps")
        lat_t = sem("lat_t")
        head_act = sem("head_act")
        head_dve = sem("head_dve")
        out_stored = sem("out_stored")
        ov = [{n: sem(f"ov{l}_{n}") for n in
               ("w_in", "slots", "idx", "xs", "xst", "xsto", "gate", "up", "silu", "h", "down", "y", "out")}
              for l in range(DEPTH)]

        block = ctx.enter_context(nc.Block())

        def fence(eng):
            eng.sem_inc(fenced[eng.engine], 1)

        LAYER_UNITS = [NG * TT + TT, MLA_H * TT + TT]
        unit0 = {(0, g): g * TT for g in range(NG)}
        unit0[(0, "mem")] = NG * TT
        unit0[(1, "mla")] = LAYER_UNITS[0]
        unit0[(1, "mem")] = LAYER_UNITS[0] + MLA_H * TT
        staged0 = {(0, g): g * TT for g in range(NG)}
        staged0[(0, "mem")] = NG * TT
        staged0[(1, "mem")] = NG * TT + TT
        DEN0 = {0: 0, "mla": TT, 1: TT + MLA_H * TT}

        def window(g, v):
            i, c = v
            if g == "mem":
                return 0, 0, 2
            if g == 0:
                return (2 * i + c) * P, 2 * i + c, 2
            if g == 1:
                return DH + (i + c // 2) * 256, (i + c // 2) * 2, 2
            return DH + (2 * i + c) * P, 2 * i + c, 1

        def pipeline(eng, step, begun=False, before_last=None):
            if not begun:
                step((0, -1), True, False, False)
            step((0, 0), True, True, False)
            step((0, 1), True, True, True)
            step((0, 2), True, True, True)
            with eng.Fori(1, (TT - 2) // 2) as i:
                step((i, 1), True, True, True)
                step((i, 2), True, True, True)
            step((0, TT - 1), False, True, True)
            if before_last:
                before_last()
            step((0, TT), False, False, True)

        def wait_tokens(eng, i, t):
            if t < TT - 1:
                eng.wait_ge(x_ready, i * (TT - 1) + t + 1)
            else:
                eng.wait_ge(x_last, i + 1)

        def plus(v, k):
            return (v[0], v[1] + k)

        def idx(v):
            return 2 * v[0] + v[1]

        def early(v, n):
            return isinstance(v[0], int) and idx(v) < n

        STORED0, STORED_PER, STORED_ALL = (0, 64, 128), (16, 16, 32), 256

        def latent_idx(v):
            return 2 * TT * v[0] + v[1]

        def projects(v):
            last_head = isinstance(v[0], int) and latent_idx(v) >= (MLA_H - 1) * TT
            return 2 <= v[1] % TT < 6 and not last_head

        def latent_pipeline(eng, step):
            step((0, -1), True, False, False)
            step((0, 0), True, True, False)
            with eng.Fori(0, MLA_H // 2 - 1) as i:
                for c in range(1, 2 * TT + 1):
                    step((i, c), True, True, True)
            i = MLA_H // 2 - 1
            for c in range(1, 2 * TT + 1):
                step((i, c), c < 2 * TT - 1, c < 2 * TT, True)

        def kv_of(layer, g):
            return (km_t, v_mem, qm_t) if g == "mem" else (k_t, v_a, q_t)

        def proj_counts():
            c, a, d = {}, 0, 0
            for g in range(NG):
                c[("A", g)] = (a, d)
                a += (9 if g == 0 else 8) + (4 if g == 0 else 0)
                d += 8
            c["B"] = (a, d)
            return c
        PC = proj_counts()
        W_PARTS = ("exp_w_gate", "exp_w_up", "exp_w_down")

        def part_slot(e_par, m):
            return (3 * e_par + m + 2) % 6

        def part_view(slot, m):
            return ring_at(16 * slot, KT, DE) if m < 2 else ring_at(16 * slot, 4, D)

        def part_src(l, m, e):
            w = io[W_PARTS[m]][l, bass.ds(e, 1)]
            return w.rearrange("a (k p) n -> p (a k) n", p=P)

        RING_USES = NE // 2

        QK_ORDER = [(part + j, h) for part in (0, 2) for h in range(2) for j in range(2)]
        MEMQ_DONE = [PC[("A", 0)][0] + 13, PC["B"][0] + 12]

        N_TABLE = N_GRP + NE + NE * NE + NCHUNK + NOVER + CAP
        ROUTE_TABLE = at(72, N_TABLE)
        T_TIEG = ROUTE_TABLE[:, 0:N_GRP]
        o0 = N_GRP
        T_TIEE = ROUTE_TABLE[:, o0:o0 + NE]
        o0 += NE
        T_TRI = ROUTE_TABLE[:, o0:o0 + NE * NE].rearrange("p (a b) -> p a b", b=NE)
        o0 += NE * NE
        T_THR = ROUTE_TABLE[:, o0:o0 + NCHUNK]
        o0 += NCHUNK
        T_CHUNK = ROUTE_TABLE[:, o0:o0 + NOVER]
        o0 += NOVER
        T_SLOT = ROUTE_TABLE[:, o0:o0 + CAP]
        hot = at(64, 2, TT, NE)
        e_masked = at(66, TT, NE)
        hot_work = at(67, 2, TT, NE)
        hot_g = at(76.75, TT, N_GRP)
        r_one = at(77, 7, TT)
        r_eg = at(77.25, TT, N_GRP)
        r_exp = at(77.5, 2, NE)
        r_chunk = at(77.75, NOVER + 1)
        rank = at(69, 2, TT)
        over_slot = at(69.25, 2, TT)
        over_tmp = at(69.5, 2, TT)
        hot_both = at(80, TT, NE)
        counts = at(81, NE)
        big_tmp = at(82, NE, NE)
        ids = at(87, 2, TT, 2)
        idx_all = at(87.25, 2, NE).bitcast(I32)
        before = at(52, TT + 1, NE)
        hot_ids = at(48, 2, TT, 2, NE)
        hot_slot = at(56, 2, TT, CAP)

        @block.sync
        def _(sp):
            def mem_loads(l):
                w = io["mem_w_kv"][l].rearrange("(k p) n -> p k n", p=P)
                sp.dma_start(mem_t[l], io["mem_t"].rearrange("(k p) n -> p k n", p=P)).then_inc(mem_in, 16)
                sp.dma_start(mem_w[l][:, :, 0:GW], w[:, :, 0:GW]).then_inc(mem_in, 16)
                sp.dma_start(mem_w[l][:, :, GW:], w[:, :, GW:]).then_inc(mem_v_in, 16)

            def group_loads(g):
                b = g % 2
                if g == 1:
                    sp.wait_ge(mem_proj, 1)
                if g == 2:
                    sp.wait_ge(dve_full, 8)
                    sp.wait_ge(act_full, 13)
                w = io["a_w_in"][0].rearrange("(k p) n -> p k n", p=P)
                def weights(j):
                    return sp.dma_start(w_a[b][:, j], w[:, :, j * NG * GW + g * GW:j * NG * GW + (g + 1) * GW])
                src = io["x_t"][g].rearrange("(k p) n -> p k n", p=P)
                first = DH + HALF
                weights(0).then_inc(w_in[b], 16)
                sp.dma_start(x_t[b][:, :, 0:first], src[:, :, 0:first]).then_inc(x_in[b], 16)
                sp.dma_start(x_t[b][:, :, first:], src[:, :, first:]).then_inc(x_rest_in[b], 16)
                weights(1).then_inc(x_rest_in[b], 16)
                weights(2).then_inc(wv_in[b], 16)
                if g == 0:
                    sp.wait_ge(mem_proj, 1)
                    sp.dma_start(w_qm_a, w[:, :, 3 * NG * GW:]).then_inc(wqm_in, 16)

            def rope_loads(g):
                if g > 0:
                    sp.wait_ge(probs_t, g * TT)
                sp.dma_start(rope_a, io["rope_a"][g].rearrange("c p n -> p c n")).then_inc(rope_in, 16)

            def mask_load(m, b, units=0):
                if units > 0:
                    sp.wait_ge(masked, units)
                sp.dma_start(masked_by[:, b], io["masks"][m]).then_inc(mask_in[b], 16)

            def store(g, v):
                u = idx(v)
                b = v[1] % 2
                sp.wait_ge(o_out, unit0[(0, g)] + u + 1)
                fence(sp)
                if g == 0:
                    sp.dma_start(og[g][bass.ds(u * P, P)], o_stage[:, b]).then_inc(o_stored[b], 16)
                elif g == 1:
                    rows = og[g].rearrange("(m r) c -> r m c", r=4)[bass.ds(v[0] + v[1] // 2, 1), P * b:P * b + P]
                    sp.dma_start(rows.rearrange("a m c -> (a m) c"), o_stage[:, b]).then_inc(o_stored[b], 16)
                else:
                    rows = og[g].rearrange("(m r) c -> r m c", r=16)
                    for rr in range(2):
                        sp.dma_start(rows[bass.ds(2 * u + rr, 1)].rearrange("a m c -> (a m) c"),
                                     o_stage[64 * rr:64 * rr + 64, b]).then_inc(o_stored[b], 16)

            mem_loads(0)
            group_loads(0)
            rope_loads(0)
            sp.dma_start(ident[:], io["ident"]).then_inc(consts_in, 16)
            sp.dma_start(tri[:], io["tri"]).then_inc(consts_in, 16)
            sp.dma_start(infos[:], io["infos"]).then_inc(infos_in, 16)
            mask_load(0, 0)
            mask_load(1, 1)
            for l in range(DEPTH):
                sp.dma_start(slot_d[l], io["nowhere"]).then_inc(slots_cleared, 16)
            group_loads(1)
            mask_load(1, 0, units=1)
            for g in range(NG):
                with sp.Fori(0, TT // 2 - 2) as i:
                    store(g, (i, 0))
                    store(g, (i, 1))
                if g == 0:
                    mask_load(2, 1, units=TT - 2)
                store(g, (0, TT - 4))
                store(g, (0, TT - 3))
                if g + 1 < NG:
                    for b in range(2):
                        mask_load(3 + b if g == 0 else 5, b, units=TT * (g + 1))
                store(g, (0, TT - 2))
                if g + 1 < NG:
                    rope_loads(g + 1)
                store(g, (0, TT - 1))
                if g == 0:
                    group_loads(2)
            sp.wait_ge(act_full, PC["B"][0])
            sp.wait_ge(dve_full, PC["B"][1])
            sp.dma_start(X, io["x"].rearrange("(t p) d -> p t d", p=P)).then_inc(x_res_in, 16)
            sp.dma_start(w_out[0], io["a_w_out"][0].rearrange("(k p) n -> p k n", p=P)).then_inc(wout_in, 16)

            def gb_loads(i, names, l):
                if i > 0:
                    sp.wait_ge(x_ready, i * (TT - 1))
                    sp.wait_ge(x_last, i)
                for c, n in enumerate(names):
                    sp.dma_start(ln_gb[:, c], io[n][l:l + 1].to_broadcast([P, D])).then_inc(gb_in, 16)

            def router_loads(l):
                if l > 0:
                    sp.wait_ge(r_ps, TT * l)
                    sp.wait_ge(r_out, TT * l)
                sp.dma_start(w_router[:, :, 0:N_GRP], io["router_w_grp"][l].rearrange("(k p) n -> p k n", p=P)).then_inc(router_in, 16)
                sp.dma_start(w_router[:, :, N_GRP:], io["router_w_exp"][l].rearrange("(k p) n -> p k n", p=P)).then_inc(router_in, 16)
                sp.dma_start(b_router[:, 0:N_GRP], io["router_b_grp"][l:l + 1].to_broadcast([P, N_GRP])).then_inc(router_in, 16)
                sp.dma_start(b_router[:, N_GRP:], io["router_b_exp"][l:l + 1].to_broadcast([P, NE])).then_inc(router_in, 16)

            gb_loads(0, ("ln_mix_g", "ln_mix_b"), 0)
            router_loads(0)
            for b in range(2):
                sp.wait_ge(o_stored[b], STORED_ALL)
            sp.wait_ge(scores, unit0[(0, "mem")])
            sp.wait_ge(pv, unit0[(0, "mem")])
            for g in range(NG):
                sp.dma_start(merged[:, :, g], og[g].rearrange("(t p) c -> p t c", p=P)).then_inc(merge_in, 16)

            def expert_phase(l):
                def part(e, b, m):
                    slot = part_slot(b, m)
                    fence(sp)
                    sp.dma_start(part_view(slot, m), part_src(l, m, e)).then_inc(ring_in[slot], 16)

                if l == 1:
                    sp.wait_ge(pv, unit0[(1, "mem")])
                part(0, 0, 0)
                part(0, 0, 1)
                sp.wait_ge(y_ps, TT * (l + 1))
                sp.dma_start(ROUTE_TABLE, io["route_table"].to_broadcast([P, N_TABLE])).then_inc(table_in, 16)
                sp.dma_start(ids, io["ids"]).then_inc(table_in, 16)
                part(0, 0, 2)
                for m in range(3):
                    part(1, 1, m)
                gb_loads(1 + 2 * l, ("ln_ffn_g", "ln_ffn_b"), l)
                with sp.Fori(0, NE // 2 - 1) as i:
                    for b in range(2):
                        e = 2 * i + 2 + b
                        for m, used in enumerate((gate_ps, up_ps, down_ps)):
                            sp.wait_ge(used, NE * l + e - 1)
                            part(e, b, m)

                if l == 0:
                    sp.wait_ge(down_ps, NE - 1)
                    mem_loads(1)
                    sp.wait_ge(gate_ps, NE)
                    w_b = io["b_w_in"][0].rearrange("(k p) n -> p k n", p=P)
                    sp.dma_start(w_in_b, w_b).then_inc(w_b_in, 16)

                o = ov[l]
                sp.wait_ge(over_done, l + 1)
                sp.wait_ge(down_ps, NE * (l + 1))
                for b in range(2):
                    sp.wait_ge(ys_out[b], 256 * (l + 1))
                n_over = sp.value_load(over_i[0:1, NOVER:NOVER + 1], min_val=0, max_val=NOVER)
                with sp.If(n_over > 0):
                    sp.wait_ge(o["slots"], 256)
                    with sp.Fori(0, n_over) as j:
                        e = sp.value_load(over_i[0:1, bass.ds(j, 1)], min_val=0, max_val=NE - 1)
                        for m in range(3):
                            sp.dma_start(part_view(m, m), part_src(l, m, e)).then_inc(o["w_in"], 16)
                        sp.dma_start(over_idx[0:CAP], slot_d[l][bass.ds(j * CAP, CAP)]).then_inc(o["idx"], 16)
                        sp.wait_ge(o["out"], 16 * j + 16)
                        fence(sp)
                with sp.Else():
                    sp.nop()
                sp.nop()

            def final_loads(l):
                for t in range(TT):
                    b = t % 2
                    if t >= 2:
                        sp.wait_ge(z_done, TT * (2 * l + 1) + t - 1)
                    for k in range(2):
                        sp.dma_start(y_in[:, b, k], y_d[l][k * S + t * P:k * S + (t + 1) * P]).then_inc(yin[b], 16)

            expert_phase(0)
            final_loads(0)
            sp.wait_ge(mem_proj, 2)
            sp.dma_start(w_v, io["b_w_kvb"][0].rearrange("p (h c) -> p h c", c=2 * DH)[:, :, DH:]).then_inc(b_in, 16)
            sp.dma_start(rope_b[DH:QKB], io["rope_b"].rearrange("c p n -> p c n")).then_inc(b_in, 16)
            sp.dma_start(rms_g[:], io["b_norms"]).then_inc(b_in, 16)

            def head_weights(h, hb, first):
                if not first:
                    sp.wait_ge(head_ps, 4 * h - 4)
                fence(sp)
                sp.dma_start(w_q_head[:, hb], io["b_w_qb"][0].rearrange("(k p) n -> p k n", p=P)[:, :, bass.ds(h * QKB, QKB)]).then_inc(hw_in[hb], 16)
                sp.dma_start(w_k_head[:, hb], io["b_w_kvb"][0][:, bass.ds(h * 2 * DH, DH)]).then_inc(hw_in[hb], 16)

            head_weights(0, 0, True)
            head_weights(1, 1, True)
            gb_loads(2, ("ln_mix_g", "ln_mix_b"), 1)
            router_loads(1)
            sp.wait_ge(act_full, PC["B"][0] + TT + 4)
            sp.dma_start(w_out[1], io["b_w_out"][0].rearrange("(k p) n -> p k n", p=P)).then_inc(wout_in, 16)
            with sp.Fori(0, MLA_H // 2 - 1) as i:
                head_weights(2 * i + 2, 0, False)
                head_weights(2 * i + 3, 1, False)
            expert_phase(1)
            final_loads(1)
            for t in range(TT):
                wait_tokens(sp, 3, t)
                sp.dma_start(io["out"][t * P:(t + 1) * P], X[:, t]).then_inc(out_stored, 16)
            sp.wait_ge(out_stored, 16 * TT)

        @block.gpsimd
        def _(pool):
            nc.gpsimd.memset(q_stage[:], 0.0).then_inc(zeroed, 1)
            nc.gpsimd.memset(ones[:], 1.0).then_inc(zeroed, 1)
            for c in (0, DH + S):
                last = nc.gpsimd.memset(k_t[:, :, c:c + DH], 0.0)
            last.then_inc(zeroed, 1)
            nc.gpsimd.memset(eps[:, 0:1], LN_EPS).then_inc(zeroed, 1)
            nc.gpsimd.memset(eps[:, 1:2], RMS_EPS).then_inc(zeroed, 1)
            pool.wait_ge(zeroed, 5)

            def stage(layer, g, v, free=True):
                q = kv_of(layer, g)[2]
                b = v[1] % 2
                if free:
                    pool.wait_ge(scores, unit0[(layer, g)] + idx(v) - 1)
                fence(pool)
                for hp in range(2):
                    last = nc.gpsimd.tensor_copy(q_stage[64 * hp:64 * hp + 64, b, hp::2, :],
                                                 q[64 * hp:64 * hp + 64, :, bass.ds(idx(v) * P, P)])
                last.then_inc(q_staged, 1)

            for g in range(NG):
                pool.wait_ge(dve_free, 8 * (g + 1))
                stage(0, g, (0, 0), free=g > 0)
                stage(0, g, (0, 1), free=g > 0)
                with pool.Fori(0, (TT - 2) // 2) as i:
                    for c in range(2):
                        stage(0, g, (i, 2 + c))

            def stage_all(layer):
                pool.wait_ge(act_free, MEMQ_DONE[layer])
                stage(layer, "mem", (0, 0))
                stage(layer, "mem", (0, 1))
                with pool.Fori(0, (TT - 2) // 2) as i:
                    stage(layer, "mem", (i, 2))
                    stage(layer, "mem", (i, 3))

            def norm_scale(i, store_to=None):
                pool.wait_ge(gb_in, 32 * (i + 1))
                for t in range(TT):
                    n = i * (TT - 1) + t + 1
                    if t < TT - 1:
                        pool.wait_ge(norm_done, i * TT + t + 1)
                        nc.gpsimd.tensor_tensor(X[:, t], X[:, t], ln_gb[:, 0], ALU.mult).then_inc(gmul_done, 1)
                        pool.wait_ge(gmul_done, n)
                        nc.gpsimd.tensor_tensor(X[:, t], X[:, t], ln_gb[:, 1], ALU.add).then_inc(x_ready, 1)
                    if store_to is not None:
                        wait_tokens(pool, i, t)
                        pool.dma_start(store_to[t * P:(t + 1) * P], X[:, t]).then_inc(x1_stored, 16)

            def experts(l):
                pool.wait_ge(r_ps, TT * (l + 1))
                nc.gpsimd.memset(xs[:], 0.0).then_inc(zeroed, 1)
                pool.wait_ge(zeroed, 6 + l)
                pool.wait_ge(x1_stored, 16 * TT * (l + 1))
                pool.wait_ge(route_done, l + 1)

                def gathers_copy(e):
                    return 2 * NE * l + (e + 1 if isinstance(e, int) and e < 2 else 2 * e - 1)

                def scatters_copy(e):
                    return 2 * NE * l + (e + NE + 1 if isinstance(e, int) and e >= NE - 2 else 2 * e + 4)

                def gather(e, n, b, first=False):
                    if not first:
                        pool.wait_ge(xs_in[b], 16 * n)
                        pool.wait_ge(xst_ps, 2 * n + b - 1)
                    nc.gpsimd.tensor_copy(g_idx[0:CAP, b:b + 1], idx_all[0:CAP, 0, bass.ds(e, 1)]).then_inc(idx_set, 1)
                    pool.wait_ge(idx_set, gathers_copy(e))
                    fence(pool)
                    pool.indirect_dma_start(xs[0:CAP, b], None, x1_d[l][:, :],
                                            bass.IndirectOffsetOnAxis(ap=g_idx[0:CAP, b:b + 1], axis=0),
                                            bounds_check=S - 1, oob_is_err=False).then_inc(xs_in[b], 16)

                def scatter(e, n, b, first=False):
                    if not first:
                        pool.wait_ge(ys_out[b], 16 * n)
                    nc.gpsimd.tensor_copy(s_idx[0:CAP, b:b + 1], idx_all[0:CAP, 1, bass.ds(e, 1)]).then_inc(idx_set, 1)
                    pool.wait_ge(idx_set, scatters_copy(e))
                    pool.wait_ge(y_act, 2 * n + b + 1)
                    pool.wait_ge(y_dve, 2 * n + b + 1)
                    fence(pool)
                    pool.indirect_dma_start(y_d[l][:, :], bass.IndirectOffsetOnAxis(ap=s_idx[0:CAP, b:b + 1], axis=0),
                                            ys[0:CAP, b], None, bounds_check=2 * S - 1, oob_is_err=False).then_inc(ys_out[b], 16)

                n0 = RING_USES * l
                gather(0, n0, 0, first=l == 0)
                gather(1, n0, 1, first=l == 0)
                for b in range(2):
                    gather(2 + b, n0 + 1, b)
                    scatter(b, n0, b, first=l == 0)
                with pool.Fori(0, NE // 2 - 2) as i:
                    for b in range(2):
                        gather(2 * i + 4 + b, n0 + i + 2, b)
                        scatter(2 * i + 2 + b, n0 + i + 1, b)
                for b in range(2):
                    scatter(NE - 2 + b, n0 + NE // 2 - 1, b)
                o = ov[l]
                pool.wait_ge(over_done, l + 1)
                n_over = pool.value_load(over_i[0:1, NOVER:NOVER + 1], min_val=0, max_val=NOVER)
                with pool.If(n_over > 0):
                    pool.wait_ge(slots_cleared, 32)
                    pool.wait_ge(infos_in, 16)
                    for t in range(TT):
                        for k in range(2):
                            pool.indirect_dma_start(slot_d[l][:, :], bass.IndirectOffsetOnAxis(ap=slots_i[:, t, k:k + 1], axis=0),
                                                    infos[:, t, k, :], None, bounds_check=SLOTS - 1, oob_is_err=False).then_inc(o["slots"], 16)
                    with pool.Fori(0, n_over) as j:
                        pool.wait_ge(o["idx"], 16 * j + 16)
                        fence(pool)
                        pool.indirect_dma_start(xs[0:CAP, 0], None, x1_d[l][:, :],
                                                bass.IndirectOffsetOnAxis(ap=over_idx[0:CAP, 0:1], axis=0),
                                                bounds_check=S - 1, oob_is_err=False).then_inc(o["xs"], 16)
                        pool.wait_ge(o["y"], j + 1)
                        fence(pool)
                        pool.indirect_dma_start(y_d[l][:, :], bass.IndirectOffsetOnAxis(ap=over_idx[0:CAP, 1:2], axis=0),
                                                ys[0:CAP, 0], None, bounds_check=2 * S - 1, oob_is_err=False).then_inc(o["out"], 16)
                with pool.Else():
                    pool.nop()
                pool.nop()

            stage_all(0)
            norm_scale(0, x1_d[0])
            experts(0)
            norm_scale(1)
            stage_all(1)
            norm_scale(2, x1_d[1])
            experts(1)
            norm_scale(3)

        @block.tensor
        def _(pe):
            def mm(out, lhsT, rhs, start=True, stop=True):
                return nc.tensor.matmul(out, lhsT, rhs, start=start, stop=stop)

            def mem_projection(l):
                pe.wait_ge(mem_in, 32 * (l + 1))
                for j in range(2):
                    for k in range(KT):
                        mm(ps[:, 6, j * MEM:(j + 1) * MEM], mem_w[l][:, k, j * P:(j + 1) * P], mem_t[l][:, k], k == 0, k == KT - 1)
                pe.wait_ge(mem_v_in, 16 * (l + 1))
                for j in range(2):
                    for k in range(KT):
                        last = mm(ps[:, 7, j * GW:(j + 1) * GW], mem_t[l][:, k, j * P:(j + 1) * P], mem_w[l][:, k, GW:], k == 0, k == KT - 1)
                last.then_inc(mem_proj, 1)

            na, nd = [0], [0]

            def for_act(cols, products):
                n = na[0]
                if n >= 2:
                    pe.wait_ge(act_free, n - 1)
                for k, (l_, r_) in enumerate(products):
                    last = mm(ps[:, 4 + n % 2, 0:cols], l_, r_, k == 0, k == len(products) - 1)
                last.then_inc(act_full, 1)
                na[0] += 1

            def for_dve(products):
                n = nd[0]
                if n >= 4:
                    pe.wait_ge(dve_free, n - 3)
                for k, (l_, r_) in enumerate(products):
                    last = mm(ps[:, n % 4, :], l_, r_, k == 0, k == KT - 1)
                last.then_inc(dve_full, 1)
                nd[0] += 1

            def group_projection(g):
                b = g % 2
                uses = g // 2 + 1
                pe.wait_ge(w_in[b], 16 * uses)
                pe.wait_ge(x_in[b], 16 * uses)
                if g > 0:
                    pe.wait_ge(o_out, g * TT)
                for n, (j, h) in enumerate(QK_ORDER):
                    if n == 2:
                        pe.wait_ge(x_rest_in[b], 32 * uses)
                    c0 = DH + h * HALF
                    for_dve([(w_a[b][:, j // 2, k, (j % 2) * P:(j % 2 + 1) * P], x_t[b][:, k, c0:c0 + HALF]) for k in range(KT)])
                pe.wait_ge(wv_in[b], 16 * uses)
                for t in range(9 if g == 0 else 8):
                    if g > 0 and t == 7:
                        attention_step(0, g)((0, -1), True, False, False)
                    c0 = t * P + (0 if g == 0 else DH)
                    for_act(GW, [(x_t[b][:, k, c0:c0 + P], w_a[b][:, 2, k]) for k in range(KT)])
                if g == 0:
                    pe.wait_ge(wqm_in, 16)
                    for j in range(2):
                        for h in range(2):
                            if j == 1 and h == 1:
                                attention_step(0, g)((0, -1), True, False, False)
                            c0 = DH + h * HALF
                            for_act(HALF, [(w_qm_a[:, k, j * P:(j + 1) * P], x_t[b][:, k, c0:c0 + HALF]) for k in range(KT)])

            def attention_step(layer, g):
                keys, vals, _ = kv_of(layer, g)
                u0 = unit0[(layer, g)]

                def step(v, ahead, now, behind):
                    if ahead:
                        w = plus(v, 1)
                        b = w[1] % 2
                        col, _, nch = window(g, w)
                        pe.wait_ge(q_staged, staged0[(layer, g)] + idx(w) + 1)
                        if u0 > 0 or not early(w, 2):
                            pe.wait_ge(probs, u0 + idx(w) - 1)
                        for h in range(GH):
                            last = mm(ps[:, 2 * b + h // 2, (h % 2) * 256:(h % 2) * 256 + nch * P], q_stage[:, b, h],
                                      keys[:, h // 2, bass.ds(col, nch * P)])
                        last.then_inc(scores, 1)
                    if now:
                        b = v[1] % 2
                        _, _, nch = window(g, v)
                        u = u0 + idx(v)
                        pe.wait_ge(probs, u + 1)
                        if u0 > 0 or not early(v, 1):
                            pe.wait_ge(pt_act, u)
                            pe.wait_ge(pt_dve, u)
                        for h in range(GH):
                            for c in range(nch):
                                last = nc.tensor.transpose(ps[:, 4 + h // 2, (h % 2) * 256 + c * P:(h % 2) * 256 + (c + 1) * P],
                                                           prob[:, b, h * 256 + c * P:h * 256 + (c + 1) * P], ident[:])
                        last.then_inc(probs_t, 1)
                    if behind:
                        w = plus(v, -1)
                        b = w[1] % 2
                        _, vt, nch = window(g, w)
                        u = u0 + idx(w)
                        pe.wait_ge(pt_act, u + 1)
                        pe.wait_ge(pt_dve, u + 1)
                        if u0 > 0 or not early(w, 2):
                            pe.wait_ge(o_out, u - 1)
                        for h in range(GH):
                            for c in range(nch):
                                last = mm(ps[:, 6 + b, h * DH:(h + 1) * DH], prob_t[:, b, h * 256 + c * P:h * 256 + (c + 1) * P],
                                          vals[:, bass.ds(vt + c, 1), h * DH:(h + 1) * DH].rearrange("p a n -> p (a n)"), c == 0, c == nch - 1)
                        last.then_inc(pv, 1)
                return step

            def group_attention(layer, g):
                step = attention_step(layer, g)
                if layer == 0 and g != "mem":
                    pe.wait_ge(act_free, PC[("A", g)][0] + (9 if g == 0 else 8))
                    pe.wait_ge(dve_free, 8 * (g + 1))
                else:
                    pe.wait_ge(mem_kv_act, layer + 1)
                    pe.wait_ge(mem_kv_dve, layer + 1)
                pipeline(pe, step, begun=layer == 0 and g != "mem")

            def out_projection(l):
                nct = 4 if l == 0 else 6
                pe.wait_ge(o_out, unit0[(l, "mem")] + TT)
                pe.wait_ge(wout_in, 16 * (l + 1))
                pe.wait_ge(router_in, 64 * (l + 1))
                n0 = l * TT

                def mix_transposes(t):
                    n = n0 + t
                    if l == 0:
                        pe.wait_ge(mix_done, t + 1)
                    if n > 0:
                        pe.wait_ge(mixt_act, n)
                    if t > 4:
                        pe.wait_ge(r_out, n - 4)
                    for c in range(nct):
                        last = nc.tensor.transpose(ps[:, 4 + c // 4, (c % 4) * P:(c % 4 + 1) * P], mix[l][:, t, c * P:(c + 1) * P], ident[:])
                    last.then_inc(mixt_ps, 1)

                def products(t):
                    n = n0 + t
                    pe.wait_ge(mixt_act, n + 1)
                    b = t % 2
                    if n >= 2:
                        pe.wait_ge(z_done, 2 * l * TT + t - 1)
                    for h in range(2):
                        for c in range(nct):
                            last = mm(ps[:, 2 * b + h], mix_t[:, b, c], w_out[l][:, c, h * HALF:(h + 1) * HALF], c == 0, c == nct - 1)
                    last.then_inc(y_ps, 1)

                mix_transposes(0)
                for t in range(TT + 3):
                    if t + 1 < TT:
                        mix_transposes(t + 1)
                    if t >= 3:
                        token_transposes(2 * l, t - 3)
                    if t < TT:
                        products(t)
                    if t >= 3:
                        router(l, t - 3)

            def token_transposes(i, t):
                n = i * TT + t
                wait_tokens(pe, i, t)
                if t == 0 and i == 0:
                    pe.wait_ge(o_out, LAYER_UNITS[0])
                if n > 0:
                    pe.wait_ge(xt_act, n)
                    pe.wait_ge(xt_dve, n)
                for k in range(KT):
                    last = nc.tensor.transpose(ps[:, 6 + k // 4, (k % 4) * P:(k % 4 + 1) * P], X[:, t, k * P:(k + 1) * P], ident[:])
                last.then_inc(xt_ps, 1)

            def router(l, t):
                pe.wait_ge(xt_act, 2 * l * TT + t + 1)
                pe.wait_ge(xt_dve, 2 * l * TT + t + 1)
                if l * TT + t > 0:
                    pe.wait_ge(r_out, l * TT + t)
                pe.wait_ge(mixt_act, l * TT + min(t + 5, TT))
                for k in range(KT):
                    last = mm(ps[:, 5, 256:256 + NR], XT[:, k, t * P:(t + 1) * P], w_router[:, k], k == 0, k == KT - 1)
                last.then_inc(r_ps, 1)

            def ranks(l):
                pe.wait_ge(route_hot, l + 1)
                def flat(v):
                    return v.rearrange("p t e -> p (t e)")
                mm(ps[:, 0, 0:TT * NE], tri[:], flat(hot_both), True, False)
                mm(ps[:, 0, 0:TT * NE], ones[:], flat(before[:, 0:TT]), False, True)
                mm(ps[:, 1, 0:NE], ones[:], before[:, TT]).then_inc(rank_ps, 1)
                for k in range(2):
                    pe.wait_ge(index_hot, 2 * l + k + 1)
                    for t in range(TT):
                        last = mm(ps[0:CAP, 2, 0:2 * NE], hot_slot[:, k, t], hot_ids[:, k, t].rearrange("p c e -> p (c e)"),
                                  k == 0 and t == 0, k == 1 and t == TT - 1)
                last.then_inc(index_ps, 1)

            def row_transposes(b):
                for k in range(KT):
                    last = nc.tensor.transpose(ps[:, k // 4, (k % 4) * CAP:(k % 4 + 1) * CAP], xs[0:CAP, b, k * P:(k + 1) * P], ident[0:CAP, 0:CAP])
                return last

            def hidden(bank, w, b):
                for f in range(4):
                    for k in range(KT):
                        last = mm(ps[:, bank, f * CAP:(f + 1) * CAP], w[:, k, f * P:(f + 1) * P], xs_t[b][:, k], k == 0, k == KT - 1)
                return last

            def down(w, b):
                for h in range(2):
                    for f in range(4):
                        last = mm(ps[0:CAP, 4 + 2 * b + h, :], h_t[b][:, f], w[:, f, h * HALF:(h + 1) * HALF], f == 0, f == 3)
                return last

            def experts(l):
                n0 = NE * l
                r0 = RING_USES * l

                def rows(e, n, b):
                    pe.wait_ge(xs_in[b], 16 * n + 16)
                    if not (isinstance(e, int) and e == 0):
                        pe.wait_ge(xst_out, n0 + e)
                    row_transposes(b).then_inc(xst_ps, 1)

                def gate(e, n, b, first=False):
                    pe.wait_ge(ring_in[part_slot(b, 0)], 16 * n + 16)
                    pe.wait_ge(xst_out, n0 + e + 1)
                    if not first:
                        pe.wait_ge(silu_done, n0 + e)
                    hidden(2, part_view(part_slot(b, 0), 0), b).then_inc(gate_ps, 1)

                def expert(e, n, b, more=True, first=False):
                    if more:
                        rows(e + 1, n + b, 1 - b)
                    pe.wait_ge(ring_in[part_slot(b, 1)], 16 * n + 16)
                    if not first:
                        pe.wait_ge(h_done, n0 + e)
                    hidden(3, part_view(part_slot(b, 1), 1), b).then_inc(up_ps, 1)
                    if more:
                        gate(e + 1, n + b, 1 - b)
                    pe.wait_ge(ring_in[part_slot(b, 2)], 16 * n + 16)
                    pe.wait_ge(h_done, n0 + e + 1)
                    if not (isinstance(e, int) and n0 + e < 2):
                        pe.wait_ge(y_act, n0 + e - 1)
                        pe.wait_ge(y_dve, n0 + e - 1)
                    down(part_view(part_slot(b, 2), 2), b).then_inc(down_ps, 1)

                pe.wait_ge(route_done, l + 1)
                rows(0, r0, 0)
                gate(0, r0, 0, first=l == 0)
                expert(0, r0, 0, first=l == 0)
                expert(1, r0, 1)
                with pe.Fori(0, NE // 2 - 2) as i:
                    expert(2 * i + 2, r0 + i + 1, 0)
                    expert(2 * i + 3, r0 + i + 1, 1)
                expert(NE - 2, r0 + NE // 2 - 1, 0)
                expert(NE - 1, r0 + NE // 2 - 1, 1, more=False)
                o = ov[l]
                pe.wait_ge(y_act, n0 + NE)
                pe.wait_ge(y_dve, n0 + NE)
                pe.wait_ge(over_done, l + 1)
                n_over = pe.value_load(over_i[0:1, NOVER:NOVER + 1], min_val=0, max_val=NOVER)
                with pe.If(n_over > 0):
                    with pe.Fori(0, n_over) as j:
                        pe.wait_ge(o["xs"], 16 * j + 16)
                        row_transposes(0).then_inc(o["xst"], 1)
                        pe.wait_ge(o["w_in"], 48 * j + 48)
                        pe.wait_ge(o["xsto"], j + 1)
                        hidden(2, part_view(0, 0), 0).then_inc(o["gate"], 1)
                        hidden(3, part_view(1, 1), 0).then_inc(o["up"], 1)
                        pe.wait_ge(o["h"], j + 1)
                        down(part_view(2, 2), 0).then_inc(o["down"], 1)
                with pe.Else():
                    pe.nop()
                pe.nop()

            def token_latents(t):
                if t == 0:
                    pe.wait_ge(w_b_in, 16)
                pe.wait_ge(xt_act, TT + t + 1)
                pe.wait_ge(xt_dve, TT + t + 1)
                for_act(LAT, [(XT[:, k, t * P:(t + 1) * P], w_in_b[:, k, 0:LAT]) for k in range(KT)])

            def latent_projection():
                for j in range(2):
                    for h in range(2):
                        for_act(HALF, [(w_in_b[:, k, LAT + j * P:LAT + (j + 1) * P], XT[:, k, h * HALF:(h + 1) * HALF]) for k in range(KT)])
                for t in range(TT):
                    pe.wait_ge(lat_scaled, t + 1)
                    if t >= 2:
                        pe.wait_ge(lat_t, t - 1)
                    bank = 2 * (t % 2)
                    for c in range(3):
                        nc.tensor.transpose(ps[:, bank, c * P:(c + 1) * P], latent[:, t, c * P:(c + 1) * P], ident[:])
                    nc.tensor.transpose(ps[0:QKB, bank + 1, 0:P], latent[:, t, LAT - QKB:LAT], ident[:]).then_inc(lat_ps, 1)
                pe.wait_ge(lat_t, TT)
                pe.wait_ge(b_in, 48)
                for t in range(TT):
                    for_act(HALF, [(ckv_t[:, t * P:(t + 1) * P], w_v.rearrange("p h c -> p (h c)"))])

            def head_projection(h, hb, j):
                if j == 0:
                    pe.wait_ge(hw_in[hb], 16 * h + 32 - 16 * hb)
                if not (isinstance(h, int) and h == 0 and j == 0):
                    pe.wait_ge(head_act, 4 * h + j)
                    pe.wait_ge(head_dve, 2 * h + min(j, 2))
                cols = slice((j % 2) * HALF, (j % 2 + 1) * HALF)
                if j < 2:
                    for k in range(2):
                        last = mm(ps[0:QKB, 7, :], w_q_head[:, hb, k], cq_t[:, k, cols], k == 0, k == 1)
                else:
                    last = mm(ps[0:DH, 7, :], w_k_head[:, hb], ckv_t[:, cols])
                last.then_inc(head_ps, 1)

            def latent_attention():
                u0 = unit0[(1, "mla")]
                pe.wait_ge(act_free, PC["B"][0] + 20)
                pe.wait_ge(k_rot_done, 1)
                for j in range(4):
                    head_projection(0, 0, j)

                def step(v, ahead, now, behind):
                    if ahead:
                        w = plus(v, 1)
                        n, b, t = latent_idx(w), w[1] % 2, w[1] % TT
                        h, hb = 2 * w[0] + w[1] // TT, (w[1] // TT) % 2
                        if t == 0:
                            pe.wait_ge(head_act, 4 * h + 4)
                            pe.wait_ge(head_dve, 2 * h + 2)
                        pe.wait_ge(probs, u0 + n - 1)
                        for c in range(2):
                            last = mm(ps[:, 2 * b + c], q_head[0:QKB, hb, t * P:(t + 1) * P], k_head[0:QKB, hb, c * HALF:(c + 1) * HALF])
                        last.then_inc(scores, 1)
                    if now:
                        n, b, t = latent_idx(v), v[1] % 2, v[1] % TT
                        pe.wait_ge(probs, u0 + n + 1)
                        pe.wait_ge(pt_act, u0 + n)
                        pe.wait_ge(pt_dve, u0 + n)
                        for c in range(TT):
                            last = nc.tensor.transpose(ps[:, 4 + c // 4, (c % 4) * P:(c % 4 + 1) * P], prob[:, b, c * P:(c + 1) * P], ident[:])
                        last.then_inc(probs_t, 1)
                        if projects(v):
                            head_projection(2 * v[0] + v[1] // TT + 1, (v[1] // TT + 1) % 2, t - 2)
                    if behind:
                        w = plus(v, -1)
                        n, b = latent_idx(w), w[1] % 2
                        h = 2 * w[0] + w[1] // TT
                        pe.wait_ge(pt_act, u0 + n + 1)
                        pe.wait_ge(pt_dve, u0 + n + 1)
                        pe.wait_ge(o_out, u0 + n)
                        for c in range(TT):
                            last = mm(ps[:, 6, b * DH:(b + 1) * DH], prob_t[:, b, c * P:(c + 1) * P], v_b[:, c, bass.ds(h * DH, DH)], c == 0, c == TT - 1)
                        last.then_inc(pv, 1)
                latent_pipeline(pe, step)

            pe.wait_ge(zeroed, 5)
            mem_projection(0)
            for g in range(NG):
                group_projection(g)
                if g == 0:
                    pe.wait_ge(consts_in, 32)
                group_attention(0, g)
            group_attention(0, "mem")
            out_projection(0)
            ranks(0)
            experts(0)
            mem_projection(1)
            pe.wait_ge(mem_kv_act, 2)
            pe.wait_ge(mem_kv_dve, 2)
            for t in range(TT + 1):
                if t < TT:
                    token_transposes(1, t)
                if t >= 1:
                    token_latents(t - 1)
            latent_projection()
            latent_attention()
            group_attention(1, "mem")
            out_projection(1)
            ranks(1)
            experts(1)

        @block.scalar
        def _(act):
            na = [0]

            def copy_out(dst):
                n = na[0]
                act.wait_ge(act_full, n + 1)
                src = ps[:, 4 + n % 2, 0:dst.shape[-1]]
                nc.scalar.copy(dst, src).then_inc(act_free, 1)
                na[0] += 1

            def mem_keys(l):
                act.wait_ge(mem_proj, l + 1)
                nc.scalar.copy(km_t[:], ps[:, 6].rearrange("p (a b) -> p a b", a=2)).then_inc(mem_kv_act, 1)

            def group_values(g):
                if g > 0:
                    act.wait_ge(pv, g * TT)
                for t in range(9 if g == 0 else 8):
                    copy_out(v_a[:, t])
                if g == 0:
                    for j in range(2):
                        for h in range(2):
                            copy_out(qm_t[:, j, h * HALF:(h + 1) * HALF])

            def group_attention(layer, g):
                u0 = unit0[(layer, g)]
                nch = window(g, (0, 0))[2]
                w = nch * P

                def step(v, ahead, now, behind):
                    if now:
                        u = u0 + idx(v)
                        b = v[1] % 2
                        act.wait_ge(probs_t, u + 1)
                        if u0 > 0 or not early(v, 2):
                            act.wait_ge(pv, u - 1)
                        if nch == 2:
                            nc.scalar.copy(prob_t[:, b, 0:HALF], ps[:, 4]).then_inc(pt_act, 1)
                        else:
                            nc.scalar.copy(prob_t[:, b, 0:HALF].rearrange("p (a b) -> p a b", a=2)[:, :, 0:P],
                                           ps[:, 4].rearrange("p (a b) -> p a b", a=2)[:, :, 0:P]).then_inc(pt_act, 1)
                    if ahead:
                        x = plus(v, 1)
                        b = x[1] % 2
                        u = u0 + idx(x)
                        act.wait_ge(max_ready, u + 1)
                        for h in range(GH):
                            p = prob[:, b, h * 256:h * 256 + w]
                            last = nc.scalar.activation(p, p, ACT.Exp, bias=neg_max[:, b, h:h + 1], scale=SCALE_A,
                                                        accum_out=stat[:, b, 1, h:h + 1])
                        last.then_inc(probs, 1)
                    if now and g != "mem":
                        u = u0 + idx(v)
                        b = v[1] % 2
                        if not (g == 0 and early(v, 2)):
                            act.wait_ge(o_stored[b], STORED0[g] + STORED_PER[g] * (v[0] + v[1] // 2))
                        act.wait_ge(probs, u + 1)
                        nc.scalar.copy(o_stage[:, b, GW:], stat[:, b].rearrange("p a h -> p (a h)")).then_inc(stat_kept, 1)
                    if behind and g != "mem":
                        x = plus(v, -1)
                        b = x[1] % 2
                        act.wait_ge(pv, u0 + idx(x) + 1)
                        nc.scalar.copy(o_stage[:, b, 0:GW], ps[:, 6 + b, 0:GW]).then_inc(o_out, 1)
                pipeline(act, step, before_last=merge_exps if (layer, g) == (0, "mem") else None)

            def merge_exps():
                act.wait_ge(merge_diff, 1)
                nc.scalar.activation(merge_e[:], merge_e[:], ACT.Exp, scale=SCALE_A).then_inc(merge_exp, 1)

            def std_and_norm(i, t):
                n = i * TT + t + 1
                act.wait_ge(mv_done, n)
                nc.scalar.activation(std[:, t:t + 1], mean_var[:, t, 1:2], ACT.Sqrt, bias=eps[:, 0:1]).then_inc(sd_done, 1)
                act.wait_ge(rs_done, n)
                nc.scalar.activation(X[:, t], X[:, t], ACT.Identity, bias=rstd[:, t, 1:2], scale=rstd[:, t, 0:1]).then_inc(norm_done, 1)

            def token_copies(i, t):
                n = i * TT + t + 1
                act.wait_ge(xt_ps, n)
                nc.scalar.copy(XT[:, 0:4, t * P:(t + 1) * P], ps[:, 6].rearrange("p (a b) -> p a b", a=4)).then_inc(xt_act, 1)

            def out_projection(l):
                nct = 4 if l == 0 else 6

                def mix_copy(t):
                    act.wait_ge(mixt_ps, l * TT + t + 1)
                    if l * TT + t >= 2:
                        act.wait_ge(y_ps, l * TT + t - 1)
                    src = ps[:, 4:6].rearrange("p a b -> p (a b)")[:, 0:nct * P]
                    nc.scalar.copy(mix_t[:, t % 2, 0:nct].rearrange("p a b -> p (a b)"), src).then_inc(mixt_act, 1)
                mix_copy(0)
                for t in range(TT + 3):
                    if t + 1 < TT:
                        mix_copy(t + 1)
                    if t >= 3:
                        token_copies(2 * l, t - 3)
                    if 1 <= t < TT + 1:
                        std_and_norm(2 * l, t - 1)

            def routing(l):
                act.wait_ge(route_exp_in, 2 * l + 1)
                nc.scalar.activation(r_eg[:], r_eg[:], ACT.Exp).then_inc(route_exp, 1)
                act.wait_ge(route_exp_in, 2 * l + 2)
                nc.scalar.activation(r_one[:, 5], r_one[:, 5], ACT.Exp).then_inc(route_exp, 1)
                act.wait_ge(x1_stored, 16 * TT * (l + 1))
                act.wait_ge(r_ps, TT * (l + 1))
                nc.scalar.activation(X, X, ACT.Copy, scale=ALPHA).then_inc(x_scaled, 1)

            def silu(b):
                return nc.scalar.activation(sil[b], ps[:, 2, 0:4 * CAP].rearrange("p (a b) -> p a b", a=4), ACT.Silu)

            def experts(l):
                n0 = NE * l
                r0 = RING_USES * l

                def silu_of(e, b):
                    act.wait_ge(gate_ps, n0 + e + 1)
                    silu(b).then_inc(silu_done, 1)

                def expert(e, b, n, more=True):
                    if more:
                        silu_of(e + 1, 1 - b)
                    act.wait_ge(down_ps, n0 + e + 1)
                    if not (isinstance(n, int) and n == 0):
                        act.wait_ge(ys_out[b], 16 * n)
                    nc.scalar.copy(ys[0:CAP, b, 0:HALF], ps[0:CAP, 4 + 2 * b]).then_inc(y_act, 1)

                silu_of(0, 0)
                expert(0, 0, r0)
                expert(1, 1, r0)
                with act.Fori(0, NE // 2 - 2) as i:
                    expert(2 * i + 2, 0, r0 + i + 1)
                    expert(2 * i + 3, 1, r0 + i + 1)
                expert(NE - 2, 0, r0 + NE // 2 - 1)
                expert(NE - 1, 1, r0 + NE // 2 - 1, more=False)
                o = ov[l]
                act.wait_ge(over_done, l + 1)
                n_over = act.value_load(over_i[0:1, NOVER:NOVER + 1], min_val=0, max_val=NOVER)
                with act.If(n_over > 0):
                    with act.Fori(0, n_over) as j:
                        act.wait_ge(o["gate"], j + 1)
                        silu(0).then_inc(o["silu"], 1)
                with act.Else():
                    act.nop()
                act.nop()

            def raw_latents(t):
                n = na[0]
                act.wait_ge(act_full, n + 1)
                bank = 4 + n % 2
                if t >= 2:
                    act.wait_ge(act_free, n - 1)
                for c, (lo, hi) in enumerate(((0, QL), (QL, QL + KVL))):
                    nc.scalar.activation(square[:, t % 2, lo:hi], ps[:, bank, lo:hi], ACT.Square, accum_out=rms_ss[:, t, c:c + 1])
                nc.scalar.copy(latent[:, t], ps[:, bank, 0:LAT]).then_inc(act_free, 1)
                na[0] += 1

            def latent_norms():
                act.wait_ge(act_free, PC["B"][0] + TT)
                for c, width in enumerate((QL, KVL)):
                    last = nc.scalar.activation(rms_ss[:, :, c], rms_ss[:, :, c], ACT.Sqrt, bias=eps[:, 1:2], scale=1.0 / width)
                last.then_inc(rms_std, 1)
                for j in range(2):
                    for h in range(2):
                        copy_out(qm_t[:, j, h * HALF:(h + 1) * HALF])
                act.wait_ge(b_in, 48)
                for t in range(TT):
                    act.wait_ge(lat_ps, t + 1)
                    bank = 2 * (t % 2)
                    for c in range(3):
                        dst = cq_t[:, c, t * P:(t + 1) * P] if c < 2 else ckv_t[:, t * P:(t + 1) * P]
                        nc.scalar.activation(dst, ps[:, bank, c * P:(c + 1) * P], ACT.Copy, scale=rms_g[:, c:c + 1])
                    nc.scalar.copy(k_rot[DH:QKB, t * P:(t + 1) * P], ps[DH:QKB, bank + 1, 0:P]).then_inc(lat_t, 1)
                for t in range(TT):
                    copy_out(v_b[:, t])

            def head_copy(h, hb, j):
                act.wait_ge(head_ps, 4 * h + j + 1)
                act.wait_ge(scores, unit0[(1, "mla")] - TT + TT * h)
                dst = (q_head if j < 2 else k_head)[0:DH, hb, (j % 2) * HALF:(j % 2 + 1) * HALF]
                nc.scalar.copy(dst, ps[0:DH, 7]).then_inc(head_act, 1)

            def latent_attention():
                u0 = unit0[(1, "mla")]
                for j in range(4):
                    head_copy(0, 0, j)

                def step(v, ahead, now, behind):
                    if ahead:
                        w = plus(v, 1)
                        n, b = latent_idx(w), w[1] % 2
                        act.wait_ge(max_ready, u0 + n + 1)
                        act.wait_ge(probs_t, u0 + n - 1)
                        nc.scalar.activation(prob[:, b], ps[:, 2 * b:2 * b + 2].rearrange("p a b -> p (a b)"), ACT.Exp,
                                             bias=neg_max[:, b, 0:1], scale=SCALE_B, accum_out=stat[:, b, 1, 0:1]).then_inc(probs, 1)
                    if now:
                        n, b = latent_idx(v), v[1] % 2
                        act.wait_ge(probs_t, u0 + n + 1)
                        act.wait_ge(pv, u0 + n - 1)
                        nc.scalar.copy(prob_t[:, b, 0:HALF], ps[:, 4]).then_inc(pt_act, 1)
                        if projects(v):
                            head_copy(2 * v[0] + v[1] // TT + 1, (v[1] // TT + 1) % 2, v[1] % TT - 2)
                latent_pipeline(act, step)

            act.wait_ge(zeroed, 5)
            mem_keys(0)
            for g in range(NG):
                group_values(g)
                group_attention(0, g)
            group_attention(0, "mem")
            out_projection(0)
            routing(0)
            experts(0)
            mem_keys(1)
            for t in range(TT + 3):
                if t < TT:
                    std_and_norm(1, t)
                if 2 <= t < TT + 2:
                    token_copies(1, t - 2)
                if t >= 3:
                    raw_latents(t - 3)
            latent_norms()
            latent_attention()
            group_attention(1, "mem")
            out_projection(1)
            routing(1)
            experts(1)
            for t in range(TT):
                std_and_norm(3, t)

        @block.vector
        def _(dve):
            def chain(s, count):
                def link(ins):
                    count[0] += 1
                    ins.then_inc(s, 1)
                    dve.wait_ge(s, count[0])
                return link

            merge_link = chain(mstep, [0])
            route_link = chain(rstep, [0])
            ln_link = chain(rs_step, [0])

            def mem_values(l):
                dve.wait_ge(mem_proj, l + 1)
                nc.vector.tensor_copy(v_mem[:], ps[:, 7].rearrange("p (a b) -> p a b", a=2)).then_inc(mem_kv_dve, 1)

            swap_a = [(i + 8) % 16 if i < 16 else i for i in range(32)]
            swap_b = [(i + 16) % 32 for i in range(32)]

            def group_rope(g):
                dve.wait_ge(rope_in, 16 * (g + 1))
                if g > 0:
                    dve.wait_ge(scores, g * TT)
                    dve.wait_ge(pv, g * TT)
                for m, (j, h) in enumerate(QK_ORDER):
                    n = g * 8 + m
                    b = n % 2
                    bank = ps[:, n % 4]
                    cols = slice(h * HALF, (h + 1) * HALF)
                    dve.wait_ge(dve_full, n + 1)
                    nc.vector.stream_shuffle(rope_tmp[:, 2 * b], bank, swap_a).then_inc(rope_a_s, 1)
                    nc.vector.tensor_tensor(rope_tmp[:, 2 * b + 1], bank, rope_a[:, 0, cols], ALU.mult).then_inc(rope_b_s, 1)
                    dve.wait_ge(rope_a_s, n + 1)
                    nc.vector.tensor_tensor(rope_tmp[:, 2 * b], rope_tmp[:, 2 * b], rope_a[:, 1, cols], ALU.mult).then_inc(rope_c_s, 1)
                    dve.wait_ge(rope_b_s, n + 1)
                    dve.wait_ge(rope_c_s, n + 1)
                    dst = q_t[:, j, cols] if j < 2 else k_t[:, j - 2, DH + h * HALF:DH + (h + 1) * HALF]
                    nc.vector.tensor_tensor(dst, rope_tmp[:, 2 * b], rope_tmp[:, 2 * b + 1], ALU.add).then_inc(dve_free, 1)

            def group_attention(layer, g):
                u0 = unit0[(layer, g)]
                nch = window(g, (0, 0))[2]
                w = nch * P

                def step(v, ahead, now, behind):
                    if ahead:
                        x = plus(v, 1)
                        b = x[1] % 2
                        u = u0 + idx(x)
                        dve.wait_ge(scores, u + 1)
                        if u0 > 0 or not early(x, 2):
                            dve.wait_ge(probs_t, u - 1)
                        if layer == 0 and not early((x[0], x[1] + u0), 2):
                            dve.wait_ge(stat_kept, u - 1 if g != "mem" else NG * TT)
                        if g != "mem":
                            if g == 0:
                                loads = (1 if early(x, 1) else 2) if b == 0 else x[0] if not early(x, TT) else 1
                            else:
                                loads = g + 2
                            dve.wait_ge(mask_in[b], 16 * loads)
                        fence(dve)
                        for h in range(GH):
                            last = nc.vector.tensor_tensor_reduce(
                                out=prob[:, b, h * 256:h * 256 + w], in0=ps[:, 2 * b + h // 2, (h % 2) * 256:(h % 2) * 256 + w],
                                in1=masked_by[:, b, 0:w], scale=1.0, scalar=LOWEST, op0=ALU.add, op1=ALU.max,
                                accum_out=stat[:, b, 0, h:h + 1])
                        last.then_inc(masked, 1)
                        dve.wait_ge(masked, staged0[(layer, g)] + idx(x) + 1)
                        nc.vector.tensor_scalar(neg_max[:, b], stat[:, b, 0], -SCALE_A, None, ALU.mult).then_inc(max_ready, 1)
                    if now:
                        u = u0 + idx(v)
                        b = v[1] % 2
                        dve.wait_ge(probs_t, u + 1)
                        if g == "mem":
                            dve.wait_ge(o_out, u - 1)
                            nc.vector.reciprocal(recip_den[:, b], stat[:, b, 1]).then_inc(den_ready, 1)
                        if u0 > 0 or not early(v, 2):
                            dve.wait_ge(pv, u - 1)
                        if nch == 2:
                            nc.vector.tensor_copy(prob_t[:, b, HALF:], ps[:, 5]).then_inc(pt_dve, 1)
                        else:
                            nc.vector.tensor_copy(prob_t[:, b, HALF:].rearrange("p (a b) -> p a b", a=2)[:, :, 0:P],
                                                  ps[:, 5].rearrange("p (a b) -> p a b", a=2)[:, :, 0:P]).then_inc(pt_dve, 1)
                    if behind and g == "mem":
                        x = plus(v, -1)
                        b = x[1] % 2
                        dve.wait_ge(pv, u0 + idx(x) + 1)
                        dve.wait_ge(den_ready, DEN0[layer] + idx(x) + 1)
                        off = GW if layer == 0 else MLA_H * DH
                        nc.vector.tensor_tensor(
                            mix[layer][:, bass.ds(idx(x), 1), off:off + GW].rearrange("p a (h c) -> p (a h) c", h=GH),
                            ps[:, 6 + b, 0:GW].rearrange("p (h c) -> p h c", h=GH),
                            recip_den[:, b].rearrange("p (h a) -> p h a", a=1).to_broadcast([P, GH, DH]), ALU.mult).then_inc(o_out, 1)
                pipeline(dve, step, before_last=merge_weights if (layer, g) == (0, "mem") else None)

            def zero_masks(l):
                dve.wait_ge(masked, staged0[(l, "mem")])
                nc.vector.memset(masked_by, 0.0).then_inc(mask_zero, 1)
                dve.wait_ge(mask_zero, l + 1)

            def merge_weights():
                dve.wait_ge(merge_in, 48)
                mx = merged[:, :, :, GW:GW + GH]
                dn = merged[:, :, :, GW + GH:]
                merge_link(nc.vector.tensor_tensor(merge_m[:], mx[:, :, 0], mx[:, :, 1], ALU.max))
                merge_link(nc.vector.tensor_tensor(merge_m[:], merge_m[:], mx[:, :, 2], ALU.max))
                for g in range(NG):
                    last = nc.vector.tensor_tensor(merge_e[:, :, g], mx[:, :, g], merge_m[:], ALU.subtract)
                last.then_inc(merge_diff, 1)
                dve.wait_ge(merge_exp, 1)
                merge_link(nc.vector.tensor_tensor(dn, dn, merge_e[:], ALU.mult))
                merge_link(nc.vector.tensor_tensor(merge_m[:], dn[:, :, 0], dn[:, :, 1], ALU.add))
                merge_link(nc.vector.tensor_tensor(merge_m[:], merge_m[:], dn[:, :, 2], ALU.add))
                merge_link(nc.vector.reciprocal(merge_m[:], merge_m[:]))
                for g in range(NG):
                    last = nc.vector.tensor_tensor(merge_e[:, :, g], merge_e[:, :, g], merge_m[:], ALU.mult)
                merge_link(last)

            def merge():
                for t in range(TT):
                    for g in range(NG):
                        o = merged[:, t, g, 0:GW].rearrange("p (h c) -> p h c", h=GH)
                        wt = merge_e[:, t, g].rearrange("p (h a) -> p h a", a=1).to_broadcast([P, GH, DH])
                        last = nc.vector.tensor_tensor(o, o, wt, ALU.mult)
                    merge_link(last)
                    m2 = mix[0][:, t, 0:GW]
                    merge_link(nc.vector.tensor_tensor(m2, merged[:, t, 0, 0:GW], merged[:, t, 1, 0:GW], ALU.add))
                    nc.vector.tensor_tensor(m2, m2, merged[:, t, 2, 0:GW], ALU.add).then_inc(mix_done, 1)

            def tile_stats(i, t):
                n = i * TT + t
                dve.wait_ge(z_done, n + 1)
                for h in range(2):
                    last = nc.vector.bn_stats(stats[:, t % 2, h], X[:, t, h * HALF:(h + 1) * HALF])
                last.then_inc(st_done, 1)
                dve.wait_ge(st_done, n + 1)
                nc.vector.bn_aggr(mean_var[:, t], stats[:, t % 2]).then_inc(mv_done, 1)

            def tile_rstd(i, t):
                dve.wait_ge(sd_done, i * TT + t + 1)
                ln_link(nc.vector.reciprocal(rstd[:, t, 0:1], std[:, t:t + 1]))
                nc.vector.scalar_tensor_tensor(out=rstd[:, t, 1:2], in0=mean_var[:, t, 0:1], scalar=-1.0, in1=rstd[:, t, 0:1],
                                               op0=ALU.mult, op1=ALU.mult).then_inc(rs_done, 1)

            def last_scale(i):
                t = TT - 1
                dve.wait_ge(gb_in, 32 * (i + 1))
                dve.wait_ge(norm_done, (i + 1) * TT)
                nc.vector.tensor_tensor(X[:, t], X[:, t], ln_gb[:, 0], ALU.mult).then_inc(last_gmul, 1)
                dve.wait_ge(last_gmul, i + 1)
                nc.vector.tensor_tensor(X[:, t], X[:, t], ln_gb[:, 1], ALU.add).then_inc(x_last, 1)

            def token_copies(i, t):
                n = i * TT + t + 1
                dve.wait_ge(xt_ps, n)
                nc.vector.tensor_copy(XT[:, 4:8, t * P:(t + 1) * P], ps[:, 7].rearrange("p (a b) -> p a b", a=4)).then_inc(xt_dve, 1)

            def out_projection(l):
                i = 2 * l
                if l == 0:
                    dve.wait_ge(x_res_in, 16)
                dve.wait_ge(router_in, 64 * (l + 1))
                for t in range(TT + 3):
                    if t >= 3:
                        token_copies(i, t - 3)
                    if t < TT:
                        dve.wait_ge(y_ps, l * TT + t + 1)
                        nc.vector.scalar_tensor_tensor(out=X[:, t], in0=X[:, t], scalar=ALPHA,
                                                       in1=ps[:, 2 * (t % 2):2 * (t % 2) + 2].rearrange("p a b -> p (a b)"),
                                                       op0=ALU.mult, op1=ALU.add).then_inc(z_done, 1)
                    if t >= 3:
                        dve.wait_ge(r_ps, l * TT + t - 2)
                        nc.vector.tensor_tensor(logits[:, t - 3], ps[:, 5, 256:256 + NR], b_router[:], ALU.add).then_inc(r_out, 1)
                    if t < TT:
                        tile_stats(i, t)
                    if 1 <= t < TT + 1:
                        tile_rstd(i, t - 1)
                    if t == TT:
                        last_scale(i)

            def routing(l):
                link = route_link
                V = nc.vector
                g_l = logits[:, :, 0:N_GRP]
                e_l = logits[:, :, N_GRP:]
                dve.wait_ge(r_out, TT * (l + 1))

                def bc(x, n):
                    return x.rearrange("p (t a) -> p t a", a=1).to_broadcast([P, TT, n])

                def first_max(src, n, tie, m, hot, scratch):
                    link(V.tensor_reduce(m, src, AX.X, ALU.max))
                    link(V.tensor_tensor(hot, src, bc(m, n), ALU.is_equal))
                    link(V.tensor_tensor(hot, hot, tie.rearrange("p (a n) -> p a n", a=1).to_broadcast([P, TT, n]), ALU.mult))
                    link(V.tensor_reduce(scratch, hot, AX.X, ALU.max))
                    link(V.tensor_tensor(hot, hot, bc(scratch, n), ALU.is_equal))

                dve.wait_ge(table_in, 32 * (l + 1))
                gm, sc, gs, m1, m2, e21, w1 = (r_one[:, n] for n in range(7))
                first_max(g_l, N_GRP, T_TIEG, gm, hot_g, sc)
                V.tensor_tensor(r_eg[:], g_l, bc(gm, N_GRP), ALU.subtract).then_inc(route_exp_in, 1)
                link(V.tensor_scalar(hot_g, hot_g, BIG, -BIG, ALU.mult, ALU.add))
                link(V.tensor_tensor(e_masked.rearrange("p t (g e) -> p t g e", g=N_GRP), e_l.rearrange("p t (g e) -> p t g e", g=N_GRP),
                                     hot_g.rearrange("p t (g a) -> p t g a", a=1).to_broadcast([P, TT, N_GRP, EPG]), ALU.add))
                first_max(e_masked, NE, T_TIEE, m1, hot[:, 0], sc)
                link(V.scalar_tensor_tensor(out=e_masked, in0=hot[:, 0], scalar=-2 * BIG, in1=e_masked, op0=ALU.mult, op1=ALU.add))
                first_max(e_masked, NE, T_TIEE, m2, hot[:, 1], sc)
                V.tensor_tensor(e21, m2, m1, ALU.subtract).then_inc(route_exp_in, 1)
                link(V.tensor_tensor(hot_both, hot[:, 0], hot[:, 1], ALU.add))
                V.memset(before[:, 0], 0.0)
                link(V.tensor_copy(before[:, 1], hot_both[:, 0]))
                for t in range(1, TT):
                    last = V.tensor_tensor(before[:, t + 1], before[:, t], hot_both[:, t], ALU.add)
                    if t < TT - 1:
                        link(last)
                last.then_inc(route_hot, 1)
                for k in range(2):
                    last = V.tensor_tensor(hot_ids[:, k], hot[:, k].rearrange("p t (a e) -> p t a e", a=1).to_broadcast([P, TT, 2, NE]),
                                           ids[:, k].rearrange("p t (c a) -> p t c a", a=1).to_broadcast([P, TT, 2, NE]), ALU.mult)
                link(last)
                dve.wait_ge(rank_ps, l + 1)
                for k in range(2):
                    last = V.tensor_tensor(hot_work[:, k], hot[:, k], ps[:, 0, 0:TT * NE].rearrange("p (t e) -> p t e", e=NE), ALU.mult)
                link(last)
                link(V.tensor_reduce(rank, hot_work, AX.X, ALU.add))
                for k in range(2):
                    V.tensor_tensor(hot_slot[:, k], bc(rank[:, k], CAP),
                                    T_SLOT.rearrange("p (a n) -> p a n", a=1).to_broadcast([P, TT, CAP]), ALU.is_equal).then_inc(index_hot, 1)
                link(V.tensor_copy(counts, ps[:, 1, 0:NE]))
                dve.wait_ge(route_exp, 2 * l + 2)
                link(V.tensor_reduce(gs, r_eg[:], AX.X, ALU.add))
                link(V.tensor_scalar(w1, e21, 1.0, None, ALU.add))
                link(V.tensor_tensor(gs, gs, w1, ALU.mult))
                link(V.reciprocal(gs, gs))
                link(V.tensor_copy(gates[:, :, 0], gs))
                link(V.tensor_tensor(gates[:, :, 1], gs, e21, ALU.mult))
                dve.wait_ge(index_ps, l + 1)
                V.tensor_scalar(idx_all[0:CAP].rearrange("p c e -> p (c e)"), ps[0:CAP, 2, 0:2 * NE], float(NOWHERE), None, ALU.add).then_inc(route_done, 1)

            def overflow_plan(l):
                link = route_link
                V = nc.vector
                r_nov, r_ovs = r_exp[:, 0], r_exp[:, 1]
                c3 = big_tmp.rearrange("p a b -> p (a b)")[:, 0:NE * NCHUNK].rearrange("p (a b) -> p a b", b=NCHUNK)
                link(V.tensor_tensor(c3, counts.rearrange("p (e a) -> p e a", a=1).to_broadcast([P, NE, NCHUNK]),
                                     T_THR.rearrange("p (a n) -> p a n", a=1).to_broadcast([P, NE, NCHUNK]), ALU.is_gt))
                link(V.tensor_reduce(r_nov, c3, AX.X, ALU.add))
                link(V.tensor_tensor(big_tmp, r_nov.rearrange("p (a e) -> p a e", a=1).to_broadcast([P, NE, NE]), T_TRI, ALU.mult))
                link(V.tensor_reduce(r_ovs, big_tmp, AX.X, ALU.add))
                link(V.tensor_tensor(r_nov, r_ovs, r_nov, ALU.add))
                c4 = big_tmp.rearrange("p a b -> p (a b)")[:, 0:NE * NOVER].rearrange("p (a b) -> p a b", b=NE)
                link(V.tensor_tensor(c4, r_nov.rearrange("p (a e) -> p a e", a=1).to_broadcast([P, NOVER, NE]),
                                     T_CHUNK.rearrange("p (n a) -> p n a", a=1).to_broadcast([P, NOVER, NE]), ALU.is_le))
                link(V.tensor_reduce(r_chunk[:, 0:NOVER], c4, AX.X, ALU.add))
                link(V.tensor_scalar(r_chunk[:, 0:NOVER], r_chunk[:, 0:NOVER], float(NE - 1), None, ALU.min))
                link(V.tensor_copy(r_chunk[:, NOVER:NOVER + 1], r_nov[:, NE - 1:NE]))
                link(V.tensor_copy(over_i[:], r_chunk[:]))
                for k in range(2):
                    last = V.tensor_tensor(hot_work[:, k], hot[:, k], r_ovs.rearrange("p (a e) -> p a e", a=1).to_broadcast([P, TT, NE]), ALU.mult)
                link(last)
                link(V.tensor_reduce(over_slot, hot_work, AX.X, ALU.add))
                link(V.scalar_tensor_tensor(out=over_slot, in0=over_slot, scalar=float(CAP), in1=rank, op0=ALU.mult, op1=ALU.add))
                link(V.tensor_scalar(over_tmp, rank, float(CAP), float(NOWHERE), ALU.is_lt, ALU.mult))
                link(V.tensor_tensor(over_slot, over_slot, over_tmp, ALU.add))
                V.tensor_scalar(slots_i[:].rearrange("p t k -> p k t"), over_slot, float(-CAP), None, ALU.add).then_inc(over_done, 1)

            def experts(l):
                n0 = NE * l
                r0 = RING_USES * l

                def rows(e, b):
                    dve.wait_ge(xst_ps, n0 + e + 1)
                    nc.vector.tensor_copy(xs_t[b].rearrange("p (a c) n -> p a (c n)", a=2), ps[:, 0:2, 0:4 * CAP]).then_inc(xst_out, 1)

                def hidden(e, b):
                    dve.wait_ge(silu_done, n0 + e + 1)
                    dve.wait_ge(up_ps, n0 + e + 1)
                    nc.vector.tensor_tensor(h_t[b], sil[b], ps[:, 3, 0:4 * CAP].rearrange("p (a b) -> p a b", a=4), ALU.mult).then_inc(h_done, 1)

                def expert(e, b, n, more):
                    if more:
                        rows(e + 1, 1 - b)
                    hidden(e, b)
                    dve.wait_ge(down_ps, n0 + e + 1)
                    if not (isinstance(n, int) and n == 0):
                        dve.wait_ge(ys_out[b], 16 * n)
                    nc.vector.tensor_copy(ys[0:CAP, b, HALF:], ps[0:CAP, 5 + 2 * b]).then_inc(y_dve, 1)

                rows(0, 0)
                rows(1, 1)
                overflow_plan(l)
                expert(0, 0, r0, False)
                expert(1, 1, r0, True)
                with dve.Fori(0, NE // 2 - 2) as i:
                    expert(2 * i + 2, 0, r0 + i + 1, True)
                    expert(2 * i + 3, 1, r0 + i + 1, True)
                expert(NE - 2, 0, r0 + NE // 2 - 1, True)
                expert(NE - 1, 1, r0 + NE // 2 - 1, False)
                o = ov[l]
                for b in range(2):
                    dve.wait_ge(ys_out[b], 16 * 16 * (l + 1))
                dve.wait_ge(over_done, l + 1)
                n_over = dve.value_load(over_i[0:1, NOVER:NOVER + 1], min_val=0, max_val=NOVER)
                with dve.If(n_over > 0):
                    with dve.Fori(0, n_over) as j:
                        dve.wait_ge(o["xst"], j + 1)
                        nc.vector.tensor_copy(xs_t[0].rearrange("p (a c) n -> p a (c n)", a=2), ps[:, 0:2, 0:4 * CAP]).then_inc(o["xsto"], 1)
                        dve.wait_ge(o["silu"], j + 1)
                        dve.wait_ge(o["up"], j + 1)
                        nc.vector.tensor_tensor(h_t[0], sil[0], ps[:, 3, 0:4 * CAP].rearrange("p (a b) -> p a b", a=4), ALU.mult).then_inc(o["h"], 1)
                        dve.wait_ge(o["down"], j + 1)
                        nc.vector.tensor_copy(ys[0:CAP, 0], ps[0:CAP, 4:6].rearrange("p a b -> p (a b)")).then_inc(o["y"], 1)
                with dve.Else():
                    dve.nop()
                dve.nop()

            def combine(l):
                i = 2 * l + 1
                dve.wait_ge(x_scaled, l + 1)
                for t in range(TT + 3):
                    if t < TT:
                        n = TT * l + t
                        b = t % 2
                        dve.wait_ge(yin[b], 32 * (4 * l + t // 2 + 1))
                        nc.vector.scalar_tensor_tensor(out=X[:, t], in0=y_in[:, b, 0], scalar=gates[:, t, 0:1], in1=X[:, t],
                                                       op0=ALU.mult, op1=ALU.add).then_inc(fz, 1)
                        dve.wait_ge(fz, n + 1)
                        nc.vector.scalar_tensor_tensor(out=X[:, t], in0=y_in[:, b, 1], scalar=gates[:, t, 1:2], in1=X[:, t],
                                                       op0=ALU.mult, op1=ALU.add).then_inc(z_done, 1)
                        tile_stats(i, t)
                        if l == 0 and t == 0:
                            mem_values(1)
                    if 1 <= t < TT + 1:
                        tile_rstd(i, t - 1)
                    if t == TT:
                        last_scale(i)
                    if l == 0 and t >= 3:
                        token_copies(i, t - 3)

            def latent_norms():
                V = nc.vector
                dve.wait_ge(rms_std, 1)
                V.reciprocal(rms_ss[:], rms_ss[:]).then_inc(rms_r, 1)
                dve.wait_ge(rms_r, 1)
                for t in range(TT):
                    V.tensor_scalar(latent[:, t, 0:QL], latent[:, t, 0:QL], rms_ss[:, t, 0:1], None, ALU.mult)
                    V.tensor_scalar(latent[:, t, QL:QL + KVL], latent[:, t, QL:QL + KVL], rms_ss[:, t, 1:2], None, ALU.mult).then_inc(lat_scaled, 1)
                dve.wait_ge(lat_t, TT)
                dve.wait_ge(b_in, 48)
                rows = slice(DH, QKB)
                step = chain(k_rot_step, [0])
                for h in range(2):
                    cols = slice(h * HALF, (h + 1) * HALF)
                    step(V.stream_shuffle(rope_tmp_b[rows, 0], k_rot[rows, cols], swap_b))
                    step(V.tensor_tensor(rope_tmp_b[rows, 0], rope_tmp_b[rows, 0], rope_b[rows, 1, cols], ALU.mult))
                    step(V.tensor_tensor(rope_tmp_b[rows, 1], k_rot[rows, cols], rope_b[rows, 0, cols], ALU.mult))
                    for hb in range(2):
                        last = V.tensor_tensor(k_head[rows, hb, cols], rope_tmp_b[rows, 0], rope_tmp_b[rows, 1], ALU.add)
                    step(last)
                V.tensor_copy(recip_den[:, 0, 0:1], rms_ss[:, 0, 0:1]).then_inc(k_rot_done, 1)

            def head_rope(h, hb, j):
                V = nc.vector
                rows, cols = slice(DH, QKB), slice(j * HALF, (j + 1) * HALF)
                n = 2 * h + j + 1
                dve.wait_ge(head_ps, 4 * h + j + 1)
                dve.wait_ge(scores, unit0[(1, "mla")] - TT + TT * h)
                fence(dve)
                V.stream_shuffle(rope_tmp_b[rows, 0], ps[rows, 7], swap_b).then_inc(hr_a, 1)
                V.tensor_tensor(rope_tmp_b[rows, 1], ps[rows, 7], rope_b[rows, 0, cols], ALU.mult).then_inc(hr_b, 1)
                dve.wait_ge(hr_a, n)
                V.tensor_tensor(rope_tmp_b[rows, 0], rope_tmp_b[rows, 0], rope_b[rows, 1, cols], ALU.mult).then_inc(hr_c, 1)
                dve.wait_ge(hr_b, n)
                dve.wait_ge(hr_c, n)
                V.tensor_tensor(q_head[rows, hb, cols], rope_tmp_b[rows, 0], rope_tmp_b[rows, 1], ALU.add).then_inc(head_dve, 1)

            def latent_attention():
                u0 = unit0[(1, "mla")]
                for j in range(2):
                    head_rope(0, 0, j)

                def step(v, ahead, now, behind):
                    if ahead:
                        w = plus(v, 1)
                        n, b = latent_idx(w), w[1] % 2
                        dve.wait_ge(scores, u0 + n + 1)
                        nc.vector.tensor_reduce(stat[:, b, 0, 0:1], ps[:, 2 * b:2 * b + 2].rearrange("p a b -> p (a b)"), AX.X, ALU.max).then_inc(row_max, 1)
                        dve.wait_ge(row_max, n + 1)
                        nc.vector.tensor_scalar(neg_max[:, b, 0:1], stat[:, b, 0, 0:1], -SCALE_B, None, ALU.mult).then_inc(max_ready, 1)
                    if now:
                        n, b = latent_idx(v), v[1] % 2
                        dve.wait_ge(probs_t, u0 + n + 1)
                        dve.wait_ge(o_out, u0 + n - 1)
                        nc.vector.reciprocal(recip_den[:, b, 0:1], stat[:, b, 1, 0:1]).then_inc(den_ready, 1)
                        dve.wait_ge(pv, u0 + n - 1)
                        nc.vector.tensor_copy(prob_t[:, b, HALF:], ps[:, 5]).then_inc(pt_dve, 1)
                        if projects(v) and v[1] % TT < 4:
                            head_rope(2 * v[0] + v[1] // TT + 1, (v[1] // TT + 1) % 2, v[1] % TT - 2)
                    if behind:
                        w = plus(v, -1)
                        n, b, t = latent_idx(w), w[1] % 2, w[1] % TT
                        h = 2 * w[0] + w[1] // TT
                        dve.wait_ge(pv, u0 + n + 1)
                        dve.wait_ge(den_ready, DEN0["mla"] + n + 1)
                        nc.vector.tensor_scalar(mix[1][:, t, bass.ds(h * DH, DH)], ps[:, 6, b * DH:(b + 1) * DH], recip_den[:, b, 0:1], None, ALU.mult).then_inc(o_out, 1)
                latent_pipeline(dve, step)

            dve.wait_ge(zeroed, 5)
            mem_values(0)
            for g in range(NG):
                group_rope(g)
                group_attention(0, g)
            zero_masks(0)
            group_attention(0, "mem")
            merge()
            out_projection(0)
            routing(0)
            experts(0)
            combine(0)
            latent_norms()
            latent_attention()
            zero_masks(1)
            group_attention(1, "mem")
            out_projection(1)
            routing(1)
            experts(1)
            combine(1)


def rope_table(dim, rows, reps, positions):
    inv = np.float32(ROPE_THETA) ** (-np.arange(0, dim, 2, dtype=np.float32) / np.float32(dim))
    ang = positions.astype(np.float32)[None, :] * inv.astype(np.float32)[:, None]
    c, s = np.cos(ang), np.sin(ang)
    cos = np.ones((rows, positions.size), np.float32)
    sin = np.zeros((rows, positions.size), np.float32)
    cos[:dim // 2], cos[dim // 2:dim] = c, c
    sin[:dim // 2], sin[dim // 2:dim] = -s, s
    return np.stack([np.tile(cos, (reps, 1)), np.tile(sin, (reps, 1))])


def group_order(g):
    dil = DIL_GROUPS[g][1]
    return np.arange(S).reshape(S // dil, dil).T.reshape(-1)


def group_masks():
    m = np.full((6, P, 256), -BIG, np.float32)
    q = np.arange(P)[:, None]
    for n, (g, u) in enumerate(((0, 0), (0, 1), (0, TT - 1), (1, 0), (1, 1), (2, 0))):
        window, dil = DIL_GROUPS[g]
        radius, length = window // (2 * dil), S // dil
        if g == 0:
            qpos, kpos, width = u * P + q, u * P - DH + np.arange(256)[None, :], 256
            ok = (np.abs(qpos - kpos) <= radius) & (kpos >= 0) & (kpos < length)
        elif g == 1:
            qpos, kpos, width = u * P + q, np.arange(256)[None, :], 256
            ok = np.abs(qpos - kpos) <= radius
        else:
            kpos, width = np.arange(P)[None, :], P
            ok = (q // length == kpos // length) & (np.abs(q - kpos) <= radius)
        m[n, :, :width][ok] = 0.0
    return m


def constants():
    tok = (np.arange(TT)[None, :, None] * P + np.arange(P)[:, None, None])
    infos = np.zeros((P, TT, 2, 2), np.int32)
    infos[..., 0] = tok
    infos[..., 1] = tok + S * np.arange(2)[None, None, :]
    ids = np.moveaxis(infos, 2, 1).astype(np.float32) - np.float32(NOWHERE)
    table = np.concatenate([
        np.arange(N_GRP, 0, -1), np.arange(NE, 0, -1),
        (np.arange(NE)[None, :] < np.arange(NE)[:, None]).astype(int).reshape(-1),
        CAP * np.arange(1, NCHUNK + 1), np.arange(NOVER), np.arange(CAP),
    ]).astype(np.float32)[None, :]
    return {
        "ident": np.eye(P, dtype=np.float32),
        "tri": (np.arange(P)[:, None] < np.arange(P)[None, :]).astype(np.float32),
        "nowhere": np.full((SLOTS, 2), NOWHERE, np.int32),
        "infos": infos,
        "ids": np.ascontiguousarray(ids),
        "route_table": table,
        "rope_a": np.stack([rope_table(DH // 4, DH, 2, group_order(g)) for g in range(NG)]),
        "rope_b": rope_table(ROPE_B, ROPE_B, 1, np.arange(S)),
        "masks": group_masks(),
    }


WEIGHTS = ("a_w_in", "a_w_out", "b_w_in", "b_w_qb", "b_w_kvb", "b_w_out", "mem_w_kv", "ln_mix_g", "ln_mix_b",
           "ln_ffn_g", "ln_ffn_b", "router_w_grp", "router_b_grp", "router_w_exp", "router_b_exp",
           "exp_w_gate", "exp_w_up", "exp_w_down")


def kernel(**inputs):
    import concourse.bacc as bacc
    from concourse.bass_utils import run_bass_kernel_spmd

    a = {n: np.ascontiguousarray(inputs[n]) for n in WEIGHTS}
    x = np.ascontiguousarray(inputs["x"])[0]
    a["x"] = x
    a["x_t"] = np.stack([np.pad(x[group_order(g)].T, ((0, 0), (DH, DH))) for g in range(NG)])
    a["mem_t"] = np.ascontiguousarray(np.asarray(inputs["mem"])[0].T)
    a["b_norms"] = np.ascontiguousarray(np.concatenate([
        np.asarray(inputs["b_q_norm"])[0].reshape(2, P), np.asarray(inputs["b_kv_norm"])[0].reshape(1, P)]).T)
    a.update(constants())
    nc = bacc.Bacc("TRN2", target_bir_lowering=False, num_devices=1)
    io, arrays = {}, {}
    for n, v in a.items():
        arrays[f"in_{n}"] = v
        io[n] = nc.dram_tensor(f"in_{n}", v.shape, mybir.dt.from_np(v.dtype), kind="ExternalInput").ap()
    io["out"] = nc.dram_tensor("out_x", (S, D), F32, kind="ExternalOutput").ap()
    build(nc, io)
    r = run_bass_kernel_spmd(nc, [arrays], core_ids=[0])
    return r.results[0]["out_x"].reshape(1, S, D)
```
